# Optimizing a Trainium2 kernel written in Bass

```python
import math
import jax, jax.numpy as jnp
from jax import lax
import numpy as np

D_MODEL = 1024
BATCH = 1
SEQ = 256
DEPTH = 4

N_MIXERS = 3
N_CONV_LAYERS = (DEPTH + 2) // 3
N_LRU_LAYERS = (DEPTH + 1) // 3
N_MLA_LAYERS = DEPTH // 3

CONV_WIDTH = 3

LRU_WIDTH = 1280
LRU_BLOCKS = 10
LRU_BLOCK_W = LRU_WIDTH // LRU_BLOCKS
LRU_CONV_WIDTH = 4
LRU_C = 8.0

MLA_HEADS = 8
Q_LORA_RANK = 384
KV_LORA_RANK = 256
QK_NOPE_DIM = 128
QK_ROPE_DIM = 64
V_HEAD_DIM = 128
ROPE_THETA = 10000.0
Q_BLOCK = 128

D_FF = ((8 * D_MODEL // 3 + 255) // 256) * 256

NORM_EPS = 1e-6


def rms_norm(x, g):
    xf = x.astype(jnp.float32)
    y = xf * lax.rsqrt(jnp.mean(xf * xf, axis=-1, keepdims=True) + NORM_EPS)
    return (y * g.astype(jnp.float32)).astype(x.dtype)

def causal_depthwise_conv(x, w):
    width, ch = w.shape
    return lax.conv_general_dilated(
        x, w[:, None, :].astype(x.dtype), window_strides=(1,),
        padding=[(width - 1, 0)], dimension_numbers=('NWC', 'WIO', 'NWC'),
        feature_group_count=ch)

def short_conv_mixer(xn, w_in, w_conv, w_out):
    b_gate, c_gate, h = jnp.split(xn @ w_in, 3, axis=-1)
    y = b_gate * causal_depthwise_conv(c_gate * h, w_conv)
    return y @ w_out

def rg_lru(xs, wa, ba, wx, bx, lam):
    bsz, seq, width = xs.shape
    xb = xs.reshape(bsz, seq, LRU_BLOCKS, LRU_BLOCK_W)
    r = jax.nn.sigmoid(jnp.einsum('bsnd,nde->bsne', xb, wa) + ba).reshape(bsz, seq, width)
    i = jax.nn.sigmoid(jnp.einsum('bsnd,nde->bsne', xb, wx) + bx).reshape(bsz, seq, width)
    log_a = LRU_C * r.astype(jnp.float32) * jax.nn.log_sigmoid(lam.astype(jnp.float32))
    a = jnp.exp(log_a)
    mult = jnp.sqrt(-jnp.expm1(2.0 * log_a))
    b = mult * (i * xs).astype(jnp.float32)

    def combine(left, right):
        a_l, b_l = left
        a_r, b_r = right
        return a_l * a_r, a_r * b_l + b_r

    _, h = lax.associative_scan(combine, (a, b), axis=1)
    return h.astype(xs.dtype)

def recurrent_mixer(xn, w_in, conv_w, conv_b, gate_a_w, gate_a_b, gate_x_w, gate_x_b, lam, w_out):
    gate_branch, rec_branch = jnp.split(xn @ w_in, 2, axis=-1)
    gate = jax.nn.gelu(gate_branch, approximate=True)
    rec = causal_depthwise_conv(rec_branch, conv_w) + conv_b
    h = rg_lru(rec, gate_a_w, gate_a_b, gate_x_w, gate_x_b, lam)
    return (gate * h) @ w_out

def apply_rope(t, cos, sin):
    half = t.shape[-1] // 2
    tf = t.astype(jnp.float32)
    t1, t2 = tf[..., :half], tf[..., half:]
    return jnp.concatenate([t1 * cos - t2 * sin, t2 * cos + t1 * sin], axis=-1).astype(t.dtype)

def mla_mixer(xn, cos, sin, w_down, q_norm, kv_norm, w_uq, w_ukv,
              qn_norm, qr_norm, kn_norm, kr_norm, w_o):
    bsz, seq, _ = xn.shape
    c = xn @ w_down
    c_q = c[..., :Q_LORA_RANK]
    c_kv = c[..., Q_LORA_RANK:Q_LORA_RANK + KV_LORA_RANK]
    k_rope = c[..., Q_LORA_RANK + KV_LORA_RANK:]

    q = (rms_norm(c_q, q_norm) @ w_uq).reshape(bsz, seq, MLA_HEADS, QK_NOPE_DIM + QK_ROPE_DIM)
    kv = (rms_norm(c_kv, kv_norm) @ w_ukv).reshape(bsz, seq, MLA_HEADS, QK_NOPE_DIM + V_HEAD_DIM)
    q_nope = rms_norm(q[..., :QK_NOPE_DIM], qn_norm)
    q_rope = apply_rope(rms_norm(q[..., QK_NOPE_DIM:], qr_norm), cos[:, :, None, :], sin[:, :, None, :])
    k_nope = rms_norm(kv[..., :QK_NOPE_DIM], kn_norm)
    v = kv[..., QK_NOPE_DIM:]
    k_rope = apply_rope(rms_norm(k_rope, kr_norm), cos, sin)

    scale = 1.0 / math.sqrt(QK_NOPE_DIM + QK_ROPE_DIM)
    n_blk = seq // Q_BLOCK

    def to_blocks(t):
        return t.reshape(bsz, n_blk, Q_BLOCK, *t.shape[2:]).transpose(1, 0, 2, 3, 4)

    k_idx = jnp.arange(seq)

    def attend(args):
        qn_b, qr_b, start = args
        s = (jnp.einsum('bqhd,bkhd->bhqk', qn_b, k_nope)
             + jnp.einsum('bqhr,bkr->bhqk', qr_b, k_rope)).astype(jnp.float32) * scale
        q_idx = start + jnp.arange(Q_BLOCK)
        mask = k_idx[None, :] <= q_idx[:, None]
        s = jnp.where(mask, s, jnp.finfo(jnp.float32).min)
        p = jax.nn.softmax(s, axis=-1).astype(v.dtype)
        return jnp.einsum('bhqk,bkhd->bqhd', p, v)

    starts = jnp.arange(n_blk, dtype=jnp.int32) * Q_BLOCK
    o = lax.map(attend, (to_blocks(q_nope), to_blocks(q_rope), starts))
    o = o.transpose(1, 0, 2, 3, 4).reshape(bsz, seq, MLA_HEADS * V_HEAD_DIM)
    return o @ w_o

def swiglu_ffn(xn, w_gu, w_down):
    gate, up = jnp.split(xn @ w_gu, 2, axis=-1)
    return (jax.nn.silu(gate) * up) @ w_down

def first_inputs(seed: int = 0) -> dict:
    key = jax.random.key(seed)
    ks = iter(jax.random.split(key, 40))
    f32 = jnp.float32
    res = (2 * DEPTH) ** -0.5

    def nrm(shape, scale):
        return jax.random.normal(next(ks), shape, f32) * scale

    def gain(shape):
        return 1.0 + 0.05 * jax.random.normal(next(ks), shape, f32)

    x = jax.random.normal(next(ks), (BATCH, SEQ, D_MODEL), f32)
    offset = jax.random.randint(next(ks), (BATCH, 1), 0, 1024, dtype=jnp.int32)
    positions = offset + jnp.arange(SEQ, dtype=jnp.int32)[None, :]

    mix_norm = gain((DEPTH, D_MODEL))

    nA = N_CONV_LAYERS
    conv_w_in = nrm((nA, D_MODEL, 3 * D_MODEL), D_MODEL ** -0.5)
    conv_w = nrm((nA, CONV_WIDTH, D_MODEL), CONV_WIDTH ** -0.5)
    conv_w_out = nrm((nA, D_MODEL, D_MODEL), D_MODEL ** -0.5 * res)

    nB = N_LRU_LAYERS
    lru_w_in = nrm((nB, D_MODEL, 2 * LRU_WIDTH), D_MODEL ** -0.5)
    lru_conv_w = nrm((nB, LRU_CONV_WIDTH, LRU_WIDTH), LRU_CONV_WIDTH ** -0.5)
    lru_conv_b = nrm((nB, LRU_WIDTH), 0.01)
    lru_gate_a_w = nrm((nB, LRU_BLOCKS, LRU_BLOCK_W, LRU_BLOCK_W), LRU_BLOCK_W ** -0.5)
    lru_gate_a_b = nrm((nB, LRU_BLOCKS, LRU_BLOCK_W), 0.01)
    lru_gate_x_w = nrm((nB, LRU_BLOCKS, LRU_BLOCK_W, LRU_BLOCK_W), LRU_BLOCK_W ** -0.5)
    lru_gate_x_b = nrm((nB, LRU_BLOCKS, LRU_BLOCK_W), 0.01)
    a0 = jax.random.uniform(next(ks), (nB, LRU_WIDTH), f32, 0.9, 0.999)
    lru_lambda = jnp.log(a0) - jnp.log1p(-a0)
    lru_w_out = nrm((nB, LRU_WIDTH, D_MODEL), LRU_WIDTH ** -0.5 * res)

    nC = N_MLA_LAYERS
    mla_w_down = nrm((nC, D_MODEL, Q_LORA_RANK + KV_LORA_RANK + QK_ROPE_DIM), D_MODEL ** -0.5)
    mla_q_norm = gain((nC, Q_LORA_RANK))
    mla_kv_norm = gain((nC, KV_LORA_RANK))
    mla_w_uq = nrm((nC, Q_LORA_RANK, MLA_HEADS * (QK_NOPE_DIM + QK_ROPE_DIM)), Q_LORA_RANK ** -0.5)
    mla_w_ukv = nrm((nC, KV_LORA_RANK, MLA_HEADS * (QK_NOPE_DIM + V_HEAD_DIM)), KV_LORA_RANK ** -0.5)
    mla_qn_norm = gain((nC, QK_NOPE_DIM))
    mla_qr_norm = gain((nC, QK_ROPE_DIM))
    mla_kn_norm = gain((nC, QK_NOPE_DIM))
    mla_kr_norm = gain((nC, QK_ROPE_DIM))
    mla_w_o = nrm((nC, MLA_HEADS * V_HEAD_DIM, D_MODEL), (MLA_HEADS * V_HEAD_DIM) ** -0.5 * res)

    ffn_norm = gain((DEPTH, D_MODEL))
    ffn_w_gu = nrm((DEPTH, D_MODEL, 2 * D_FF), D_MODEL ** -0.5)
    ffn_w_down = nrm((DEPTH, D_FF, D_MODEL), D_FF ** -0.5 * res)

    return {'x': x, 'positions': positions, 'mix_norm': mix_norm,
            'conv_w_in': conv_w_in, 'conv_w': conv_w, 'conv_w_out': conv_w_out,
            'lru_w_in': lru_w_in, 'lru_conv_w': lru_conv_w, 'lru_conv_b': lru_conv_b,
            'lru_gate_a_w': lru_gate_a_w, 'lru_gate_a_b': lru_gate_a_b,
            'lru_gate_x_w': lru_gate_x_w, 'lru_gate_x_b': lru_gate_x_b,
            'lru_lambda': lru_lambda, 'lru_w_out': lru_w_out,
            'mla_w_down': mla_w_down, 'mla_q_norm': mla_q_norm, 'mla_kv_norm': mla_kv_norm,
            'mla_w_uq': mla_w_uq, 'mla_w_ukv': mla_w_ukv,
            'mla_qn_norm': mla_qn_norm, 'mla_qr_norm': mla_qr_norm,
            'mla_kn_norm': mla_kn_norm, 'mla_kr_norm': mla_kr_norm, 'mla_w_o': mla_w_o,
            'ffn_norm': ffn_norm, 'ffn_w_gu': ffn_w_gu, 'ffn_w_down': ffn_w_down}

def first_block(x, positions, mix_norm, conv_w_in, conv_w, conv_w_out,
              lru_w_in, lru_conv_w, lru_conv_b, lru_gate_a_w, lru_gate_a_b,
              lru_gate_x_w, lru_gate_x_b, lru_lambda, lru_w_out,
              mla_w_down, mla_q_norm, mla_kv_norm, mla_w_uq, mla_w_ukv,
              mla_qn_norm, mla_qr_norm, mla_kn_norm, mla_kr_norm, mla_w_o,
              ffn_norm, ffn_w_gu, ffn_w_down):
    inv_freq = ROPE_THETA ** (-jnp.arange(0, QK_ROPE_DIM, 2, dtype=jnp.float32) / QK_ROPE_DIM)
    angle = positions.astype(jnp.float32)[..., None] * inv_freq
    cos, sin = jnp.cos(angle), jnp.sin(angle)

    h = x
    for i in range(DEPTH):
        kind, j = i % N_MIXERS, i // N_MIXERS
        xn = rms_norm(h, mix_norm[i])
        if kind == 0:
            y = short_conv_mixer(xn, conv_w_in[j], conv_w[j], conv_w_out[j])
        elif kind == 1:
            y = recurrent_mixer(xn, lru_w_in[j], lru_conv_w[j], lru_conv_b[j],
                                lru_gate_a_w[j], lru_gate_a_b[j], lru_gate_x_w[j],
                                lru_gate_x_b[j], lru_lambda[j], lru_w_out[j])
        else:
            y = mla_mixer(xn, cos, sin, mla_w_down[j], mla_q_norm[j], mla_kv_norm[j],
                          mla_w_uq[j], mla_w_ukv[j], mla_qn_norm[j], mla_qr_norm[j],
                          mla_kn_norm[j], mla_kr_norm[j], mla_w_o[j])
        h = h + y
        h = h + swiglu_ffn(rms_norm(h, ffn_norm[i]), ffn_w_gu[i], ffn_w_down[i])
    return h


DEPTH_2 = 2

GRID_W = 64
CTX_LEN = 256
N_MIXERS_2 = 2
N_ATT_LAYERS = (DEPTH_2 + 1) // 2
N_MLSTM_LAYERS = DEPTH_2 // 2
ATT_HEADS = 8
ATT_KV_HEADS = 2
ATT_GROUP = ATT_HEADS // ATT_KV_HEADS
ATT_HEAD_DIM = D_MODEL // ATT_HEADS
ROPE_PAIRS_PER_AXIS = ATT_HEAD_DIM // 4
MLSTM_HEADS = 4
MLSTM_V_DIM = D_MODEL // MLSTM_HEADS
MLSTM_QK_DIM = MLSTM_V_DIM // 2
MLSTM_CONV_W = 3
MLSTM_CHUNK = 64
D_FF_2 = 2816
N_MOD = 9
DEEPNORM_ALPHA = (2.0 * DEPTH_2) ** 0.25
DEEPNORM_BETA = (8.0 * DEPTH_2) ** -0.25
LN_EPS = 1e-5
RMS_EPS = 1e-6


def layer_norm(x, g, b):
    xf = x.astype(jnp.float32)
    mu = jnp.mean(xf, axis=-1, keepdims=True)
    var = jnp.mean(jnp.square(xf - mu), axis=-1, keepdims=True)
    return ((xf - mu) * lax.rsqrt(var + LN_EPS) * g + b).astype(x.dtype)

def rms_norm_2(x, g):
    xf = x.astype(jnp.float32)
    return (xf * lax.rsqrt(jnp.mean(jnp.square(xf), axis=-1, keepdims=True) + RMS_EPS) * g).astype(x.dtype)

def modulate(h, shift, scale):
    return h * (1.0 + scale) + shift

def post_norm(h, delta, g, b):
    return layer_norm(DEEPNORM_ALPHA * h + delta, g, b)

def half_ffn(h, shift, scale, gate, w_in, w_out, g, b):
    xm = modulate(h, shift, scale)
    a, u = jnp.split(xm @ w_in, 2, axis=-1)
    y = (jax.nn.silu(a) * u) @ w_out
    return post_norm(h, 0.5 * gate * y, g, b)

def axial_rope_tables(n_tokens):
    rows = n_tokens // GRID_W
    row = jnp.repeat(jnp.arange(rows, dtype=jnp.int32), GRID_W).astype(jnp.float32)
    col = jnp.tile(jnp.arange(GRID_W, dtype=jnp.int32), rows).astype(jnp.float32)
    inv = ROPE_THETA ** (-jnp.arange(ROPE_PAIRS_PER_AXIS, dtype=jnp.float32) / ROPE_PAIRS_PER_AXIS)
    ang = jnp.stack([row[:, None] * inv, col[:, None] * inv], axis=1)
    return jnp.cos(ang), jnp.sin(ang)

def apply_rope_2(x, cos, sin):
    B, L, H, Dh = x.shape
    xr = x.reshape(B, L, H, 2, 2, ROPE_PAIRS_PER_AXIS)
    x1, x2 = xr[..., 0, :], xr[..., 1, :]
    c = cos[None, :, None]
    s = sin[None, :, None]
    out = jnp.stack([x1 * c - x2 * s, x2 * c + x1 * s], axis=-2)
    return out.reshape(B, L, H, Dh).astype(x.dtype)

def gqa_softmax(q, k, v):
    s = jnp.einsum('bqhgd,bkhd->bhgqk', q, k).astype(jnp.float32) * (ATT_HEAD_DIM ** -0.5)
    p = jax.nn.softmax(s, axis=-1).astype(v.dtype)
    return jnp.einsum('bhgqk,bkhd->bqhgd', p, v)

def attention_mixer(xl, xc, cos, sin, w_in, q_gain, k_gain, w_out, need_ctx):
    def proj(xs):
        B, L, _ = xs.shape
        p = xs @ w_in
        q, k, v = jnp.split(p, [ATT_HEADS * ATT_HEAD_DIM, (ATT_HEADS + ATT_KV_HEADS) * ATT_HEAD_DIM], axis=-1)
        q = rms_norm_2(q.reshape(B, L, ATT_HEADS, ATT_HEAD_DIM), q_gain)
        k = rms_norm_2(k.reshape(B, L, ATT_KV_HEADS, ATT_HEAD_DIM), k_gain)
        v = v.reshape(B, L, ATT_KV_HEADS, ATT_HEAD_DIM)
        return q, k, v

    ql, kl, vl = proj(xl)
    qc, kc, vc = proj(xc)
    ql = apply_rope_2(ql, cos, sin)
    kl = apply_rope_2(kl, cos, sin)
    B, L = xl.shape[0], xl.shape[1]
    k_all = jnp.concatenate([kl, kc], axis=1)
    v_all = jnp.concatenate([vl, vc], axis=1)
    nb = L // Q_BLOCK
    qb = jnp.moveaxis(ql.reshape(B, nb, Q_BLOCK, ATT_KV_HEADS, ATT_GROUP, ATT_HEAD_DIM), 1, 0)
    ob = lax.map(lambda qblk: gqa_softmax(qblk, k_all, v_all), qb)
    o_lat = jnp.moveaxis(ob, 0, 1).reshape(B, L, D_MODEL) @ w_out
    o_ctx = None
    if need_ctx:
        Lc = xc.shape[1]
        oc = gqa_softmax(qc.reshape(B, Lc, ATT_KV_HEADS, ATT_GROUP, ATT_HEAD_DIM), kc, vc)
        o_ctx = oc.reshape(B, Lc, D_MODEL) @ w_out
    return o_lat, o_ctx

def centred_conv(a, w, b):
    L = a.shape[1]
    pad = MLSTM_CONV_W // 2
    ap = jnp.pad(a, ((0, 0), (pad, pad), (0, 0)))
    out = ap[:, 0:L] * w[0]
    for j in range(1, MLSTM_CONV_W):
        out = out + ap[:, j:j + L] * w[j]
    return out + b

def mlstm_scan(q, k, v, log_i, log_f, state):
    B, H, L, dk = q.shape
    dv = v.shape[-1]
    Lc = MLSTM_CHUNK
    nc = L // Lc

    def chunks(a):
        return jnp.moveaxis(a.reshape((B, H, nc, Lc) + a.shape[3:]), 2, 0)

    tri = jnp.tril(jnp.ones((Lc, Lc), dtype=bool))

    def step(carry, inp):
        C, n, m = carry
        qc, kc, vc, ic, fc = inp
        bcum = jnp.cumsum(fc, axis=-1)
        d = jnp.where(tri, bcum[..., :, None] - bcum[..., None, :] + ic[..., None, :], -jnp.inf)
        inter = m[..., None] + bcum
        m_t = jnp.maximum(inter, jnp.max(d, axis=-1))
        w_intra = jnp.exp(d - m_t[..., None])
        w_inter = jnp.exp(inter - m_t)
        s = jnp.einsum('bhtd,bhsd->bhts', qc, kc) * w_intra
        num = jnp.einsum('bhts,bhsv->bhtv', s, vc) + w_inter[..., None] * jnp.einsum('bhvd,bhtd->bhtv', C, qc)
        den = jnp.sum(s, axis=-1) + w_inter * jnp.einsum('bhd,bhtd->bht', n, qc)
        h = num / jnp.maximum(jnp.abs(den), jnp.exp(-m_t))[..., None]
        b_last = bcum[..., -1]
        d_last = b_last[..., None] - bcum + ic
        m_new = jnp.maximum(m + b_last, jnp.max(d_last, axis=-1))
        wk = jnp.exp(d_last - m_new[..., None])
        decay = jnp.exp(m + b_last - m_new)
        C_new = decay[..., None, None] * C + jnp.einsum('bhs,bhsv,bhsd->bhvd', wk, vc, kc)
        n_new = decay[..., None] * n + jnp.einsum('bhs,bhsd->bhd', wk, kc)
        return (C_new, n_new, m_new), h

    final, hs = lax.scan(step, state, (chunks(q), chunks(k), chunks(v), chunks(log_i), chunks(log_f)))
    h = jnp.moveaxis(hs, 0, 2).reshape(B, H, L, dv)
    return h, final

def mlstm_mixer(xl, xc, w_in, gate_b, conv_w, conv_b, norm_g, w_out, need_ctx):
    HQK = MLSTM_HEADS * MLSTM_QK_DIM
    HV = MLSTM_HEADS * MLSTM_V_DIM

    def proj(xs):
        B, L, _ = xs.shape
        p = xs @ w_in
        qk, v, o, g = jnp.split(p, [2 * HQK, 2 * HQK + HV, 2 * HQK + HV + D_MODEL], axis=-1)
        qk = jax.nn.silu(centred_conv(qk, conv_w, conv_b))
        q, k = jnp.split(qk, 2, axis=-1)

        def heads(a, dh):
            return jnp.transpose(a.reshape(B, L, MLSTM_HEADS, dh), (0, 2, 1, 3)).astype(jnp.float32)

        q = heads(q, MLSTM_QK_DIM)
        k = heads(k, MLSTM_QK_DIM) * (MLSTM_QK_DIM ** -0.5)
        v = heads(v, MLSTM_V_DIM)
        g = jnp.transpose((g.astype(jnp.float32) + gate_b).reshape(B, L, 4, MLSTM_HEADS), (2, 0, 3, 1))
        return q, k, v, g, o

    def zero_state(B):
        return (jnp.zeros((B, MLSTM_HEADS, MLSTM_V_DIM, MLSTM_QK_DIM), jnp.float32),
                jnp.zeros((B, MLSTM_HEADS, MLSTM_QK_DIM), jnp.float32),
                jnp.zeros((B, MLSTM_HEADS), jnp.float32))

    def flip(a):
        return jnp.flip(a, axis=2)

    def readout(h, o, dtype):
        B, H, L, dv = h.shape
        mu = jnp.mean(h, axis=-1, keepdims=True)
        var = jnp.mean(jnp.square(h - mu), axis=-1, keepdims=True)
        hn = (h - mu) * lax.rsqrt(var + LN_EPS)
        hn = jnp.transpose(hn, (0, 2, 1, 3)).reshape(B, L, D_MODEL) * norm_g
        return (hn * jax.nn.sigmoid(o.astype(jnp.float32))).astype(dtype) @ w_out

    ql, kl, vl, gl, ol = proj(xl)
    qc, kc, vc, gc, oc = proj(xc)
    B = xl.shape[0]
    hc_f, st_f = mlstm_scan(qc, kc, vc, gc[0], jax.nn.log_sigmoid(gc[1]), zero_state(B))
    hl_f, _ = mlstm_scan(ql, kl, vl, gl[0], jax.nn.log_sigmoid(gl[1]), st_f)
    hc_b, st_b = mlstm_scan(flip(qc), flip(kc), flip(vc), flip(gc[2]), jax.nn.log_sigmoid(flip(gc[3])), zero_state(B))
    hl_b, _ = mlstm_scan(flip(ql), flip(kl), flip(vl), flip(gl[2]), jax.nn.log_sigmoid(flip(gl[3])), st_b)
    o_lat = readout(hl_f + flip(hl_b), ol, xl.dtype)
    o_ctx = readout(hc_f + flip(hc_b), oc, xc.dtype) if need_ctx else None
    return o_lat, o_ctx

def second_inputs(seed: int = 0) -> dict:
    key = jax.random.key(seed)
    ks = jax.random.split(key, 24)
    D = D_MODEL
    HQK = MLSTM_HEADS * MLSTM_QK_DIM
    HV = MLSTM_HEADS * MLSTM_V_DIM
    att_cols = (ATT_HEADS + 2 * ATT_KV_HEADS) * ATT_HEAD_DIM
    ml_cols = 2 * HQK + HV + D + 4 * MLSTM_HEADS

    def nrm(k, shape, scale):
        return jax.random.normal(k, shape, jnp.float32) * scale

    forget_b = jnp.linspace(3.0, 6.0, MLSTM_HEADS, dtype=jnp.float32)
    gnoise = nrm(ks[15], (N_MLSTM_LAYERS, 4, MLSTM_HEADS), 0.1)
    gate_b = gnoise + jnp.stack([jnp.zeros_like(forget_b), forget_b, jnp.zeros_like(forget_b), forget_b], axis=0)[None]
    return {
        "x": nrm(ks[0], (BATCH, SEQ, D), 1.0),
        "c": nrm(ks[1], (BATCH, D), 1.0),
        "ctx": nrm(ks[2], (BATCH, CTX_LEN, D), 1.0),
        "c_ctx": nrm(ks[3], (D,), 1.0),
        "ada_w": nrm(ks[4], (DEPTH_2, D, N_MOD * D), 0.5 * D ** -0.5),
        "ada_b": nrm(ks[5], (DEPTH_2, N_MOD * D), 0.02),
        "ln_g": 1.0 + nrm(ks[6], (DEPTH_2, 3, D), 0.02),
        "ln_b": nrm(ks[7], (DEPTH_2, 3, D), 0.02),
        "ffn_w_in": nrm(ks[8], (DEPTH_2, 2, D, 2 * D_FF_2), D ** -0.5),
        "ffn_w_out": nrm(ks[9], (DEPTH_2, 2, D_FF_2, D), DEEPNORM_BETA * D_FF_2 ** -0.5),
        "att_w_in": nrm(ks[10], (N_ATT_LAYERS, D, att_cols), D ** -0.5),
        "att_q_gain": 1.0 + nrm(ks[11], (N_ATT_LAYERS, ATT_HEAD_DIM), 0.02),
        "att_k_gain": 1.0 + nrm(ks[12], (N_ATT_LAYERS, ATT_HEAD_DIM), 0.02),
        "att_w_out": nrm(ks[13], (N_ATT_LAYERS, D, D), DEEPNORM_BETA * D ** -0.5),
        "ml_w_in": nrm(ks[14], (N_MLSTM_LAYERS, D, ml_cols), D ** -0.5),
        "ml_gate_b": gate_b.reshape(N_MLSTM_LAYERS, 4 * MLSTM_HEADS),
        "ml_conv_w": nrm(ks[16], (N_MLSTM_LAYERS, MLSTM_CONV_W, 2 * HQK), MLSTM_CONV_W ** -0.5),
        "ml_conv_b": nrm(ks[17], (N_MLSTM_LAYERS, 2 * HQK), 0.02),
        "ml_norm_g": 1.0 + nrm(ks[18], (N_MLSTM_LAYERS, D), 0.02),
        "ml_w_out": nrm(ks[19], (N_MLSTM_LAYERS, D, D), DEEPNORM_BETA * D ** -0.5),
    }

def second_block(x, c, ctx, c_ctx, ada_w, ada_b, ln_g, ln_b, ffn_w_in, ffn_w_out,
              att_w_in, att_q_gain, att_k_gain, att_w_out,
              ml_w_in, ml_gate_b, ml_conv_w, ml_conv_b, ml_norm_g, ml_w_out):
    n_lat = x.shape[1]
    cos, sin = axial_rope_tables(n_lat)
    h_lat, h_ctx = x, ctx
    for i in range(DEPTH_2):
        need_ctx = i < DEPTH_2 - 1
        mod_lat = jnp.split((jax.nn.silu(c) @ ada_w[i] + ada_b[i])[:, None, :], N_MOD, axis=-1)
        mod_ctx = jnp.split((jax.nn.silu(c_ctx) @ ada_w[i] + ada_b[i])[None, None, :], N_MOD, axis=-1)
        h_lat = half_ffn(h_lat, mod_lat[0], mod_lat[1], mod_lat[2], ffn_w_in[i, 0], ffn_w_out[i, 0], ln_g[i, 0], ln_b[i, 0])
        h_ctx = half_ffn(h_ctx, mod_ctx[0], mod_ctx[1], mod_ctx[2], ffn_w_in[i, 0], ffn_w_out[i, 0], ln_g[i, 0], ln_b[i, 0])
        xm_lat = modulate(h_lat, mod_lat[3], mod_lat[4])
        xm_ctx = modulate(h_ctx, mod_ctx[3], mod_ctx[4])
        j = i // N_MIXERS_2
        if i % N_MIXERS_2 == 0:
            o_lat, o_ctx = attention_mixer(xm_lat, xm_ctx, cos, sin, att_w_in[j], att_q_gain[j], att_k_gain[j],
                                           att_w_out[j], need_ctx)
        else:
            o_lat, o_ctx = mlstm_mixer(xm_lat, xm_ctx, ml_w_in[j], ml_gate_b[j], ml_conv_w[j], ml_conv_b[j],
                                       ml_norm_g[j], ml_w_out[j], need_ctx)
        h_lat = post_norm(h_lat, mod_lat[5] * o_lat, ln_g[i, 1], ln_b[i, 1])
        h_lat = half_ffn(h_lat, mod_lat[6], mod_lat[7], mod_lat[8], ffn_w_in[i, 1], ffn_w_out[i, 1], ln_g[i, 2], ln_b[i, 2])
        if need_ctx:
            h_ctx = post_norm(h_ctx, mod_ctx[5] * o_ctx, ln_g[i, 1], ln_b[i, 1])
            h_ctx = half_ffn(h_ctx, mod_ctx[6], mod_ctx[7], mod_ctx[8], ffn_w_in[i, 1], ffn_w_out[i, 1], ln_g[i, 2], ln_b[i, 2])
    return h_lat


def setup_inputs(seed=0):
    out = dict(first_inputs(seed))
    for name, value in second_inputs(seed + 1).items():
        if name != "x":
            out[name + "_2"] = value
    return out


def reference(
    x, positions, mix_norm, conv_w_in, conv_w, conv_w_out, lru_w_in, lru_conv_w, lru_conv_b,
    lru_gate_a_w, lru_gate_a_b, lru_gate_x_w, lru_gate_x_b, lru_lambda, lru_w_out, mla_w_down,
    mla_q_norm, mla_kv_norm, mla_w_uq, mla_w_ukv, mla_qn_norm, mla_qr_norm, mla_kn_norm,
    mla_kr_norm, mla_w_o, ffn_norm, ffn_w_gu, ffn_w_down, c_2, ctx_2, c_ctx_2, ada_w_2, ada_b_2,
    ln_g_2, ln_b_2, ffn_w_in_2, ffn_w_out_2, att_w_in_2, att_q_gain_2, att_k_gain_2,
    att_w_out_2, ml_w_in_2, ml_gate_b_2, ml_conv_w_2, ml_conv_b_2, ml_norm_g_2, ml_w_out_2,
):
    x = first_block(
        x, positions, mix_norm, conv_w_in, conv_w, conv_w_out, lru_w_in, lru_conv_w, lru_conv_b,
        lru_gate_a_w, lru_gate_a_b, lru_gate_x_w, lru_gate_x_b, lru_lambda, lru_w_out,
        mla_w_down, mla_q_norm, mla_kv_norm, mla_w_uq, mla_w_ukv, mla_qn_norm, mla_qr_norm,
        mla_kn_norm, mla_kr_norm, mla_w_o, ffn_norm, ffn_w_gu, ffn_w_down,
    )
    return second_block(
        x, c_2, ctx_2, c_ctx_2, ada_w_2, ada_b_2, ln_g_2, ln_b_2, ffn_w_in_2, ffn_w_out_2,
        att_w_in_2, att_q_gain_2, att_k_gain_2, att_w_out_2, ml_w_in_2, ml_gate_b_2,
        ml_conv_w_2, ml_conv_b_2, ml_norm_g_2, ml_w_out_2,
    )


_drawn_inputs = setup_inputs


def setup_inputs(seed=0):
    import zlib

    import numpy as np

    out = dict(_drawn_inputs(seed))
    spreads = {}
    factors = {'lru_conv_b': 8.0,
     'lru_gate_a_b': 8.0,
     'lru_gate_x_b': 8.0,
     'mla_q_norm': 8.0,
     'mla_kv_norm': 8.0,
     'mla_qn_norm': 8.0,
     'mla_qr_norm': 8.0,
     'mla_kn_norm': 8.0,
     'mla_kr_norm': 8.0,
     'ctx_2': 5.026,
     'ada_b_2': 6.459,
     'att_q_gain_2': 25.854,
     'att_k_gain_2': 26.404,
     'ml_conv_w_2': 2.725,
     'ml_conv_b_2': 64.0,
     'ml_norm_g_2': 47.738}
    for name, (base, spread) in spreads.items():
        noise = np.random.default_rng([zlib.crc32(name.encode()), seed]).standard_normal(out[name].shape)
        drawn = base * np.exp(spread * noise) if base else spread * noise
        out[name] = __import__('jax').numpy.asarray(drawn.astype(out[name].dtype))
    for name, factor in factors.items():
        out[name] = (out[name] * factor).astype(out[name].dtype)
    return out
```

```python
from contextlib import ExitStack
import math

import numpy as np

import concourse.bass as bass
from concourse import mybir

P = 128
D = 1024
T = 256
T2 = 2 * T
KD = D // P
FF = 2816
KF = FF // P
LRU = 1280
KL = LRU // P
DEPTH, DEPTH_2 = 4, 2
HEADS, ROPE, NOPE = 8, 64, 128
Q_RANK, KV_RANK = 384, 256
N_MOD = 9
ALPHA = (2.0 * DEPTH_2) ** 0.25
NORM_EPS, LN_EPS = 1e-6, 1e-5
BIG = 1e30

SLOTS = 4
CHUNK = 8
AHEAD = 3
BANKS = 4

ALU = mybir.AluOpType
ACT = mybir.ActivationFunctionType
AX = mybir.AxisListType
F32 = mybir.dt.float32
F32R = mybir.dt.float32r
I32 = mybir.dt.int32

PARAM_SIZES = dict(
    mix_norm=DEPTH * KD, ffn_norm=DEPTH * KD, conv_w=2 * KD * 3,
    lru_conv_w=KL * 4, lru_conv_b=KL, gate_a_b=KL, gate_x_b=KL, lam=KL,
    q_norm=3, kv_norm=2, qn_norm=1, qr_norm=1, kn_norm=1, kr_norm=1,
    ada_b=2 * 72, ln_g=2 * 3 * KD, ln_b=2 * 3 * KD, att_q_gain=1, att_k_gain=1,
    ml_conv_w=8 * 3, ml_conv_b=8, ml_norm_g=KD, ml_bias_i=1, ml_bias_f=1, cond=KD * 2,
)
PARAM_AT = {}
_n = 0
for _name, _size in PARAM_SIZES.items():
    PARAM_AT[_name] = _n
    _n += _size
N_PARAM = _n

CONST_SIZES = dict(ident=P, ones=P, rot=P, sel=63, sel2=64, eps=1, eps_ln=1, inv_freq=1, row_scale=1)
CONST_AT = {}
_n = 0
for _name, _size in CONST_SIZES.items():
    CONST_AT[_name] = _n
    _n += _size
N_CONST = _n
N_MLA_CONST = 5 * P + 2 * P
N_ML_CONST = 3 * P


class Product:

    def __init__(self, name, outs, ktiles, width, weights, row=0, cuts=None, per_chunk=1, split=True,
                 cols=None, readers=None):
        self.name, self.outs, self.ktiles, self.width = name, outs, ktiles, width
        self.weights, self.row, self.split = weights, row, split
        self.cuts = cuts or [(0, ktiles)]
        self.per_chunk = per_chunk
        self.cols = cols
        self.readers = readers or ["dve"] * outs
        if per_chunk > 1:
            self.n_chunks = -(-outs // per_chunk)
        else:
            self.n_chunks = outs * len(self.cuts)

    def chunk_of(self, o):
        if self.per_chunk > 1:
            return [o // self.per_chunk]
        n = len(self.cuts)
        return list(range(o * n, o * n + n))

    def tiles_of(self, j):
        if self.per_chunk > 1:
            return [(o, k) for o in range(j * self.per_chunk, min((j + 1) * self.per_chunk, self.outs))
                    for k in range(self.ktiles)]
        n = len(self.cuts)
        return [(j // n, k) for k in range(*self.cuts[j % n])]


FF_CUTS = [(0, 6), (6, 12), (12, 17), (17, 22)]
LRU_CUTS = [(0, 5), (5, 10)]
GU_READERS = ["act", "dve"] * KF


def plan():
    s = []
    for i in range(DEPTH):
        kind, j = i % 3, i // 3
        if kind == 0:
            for part, name in enumerate(("conv_c", "conv_h", "conv_b")):
                s.append(Product(name, KD, KD, T, "w_conv_in", row=(3 * j + part) * KD))
            s.append(Product("conv_out", KD, KD, T, "w_conv_out", row=j * KD))
        elif kind == 1:
            s.append(Product("lru_rec", KL, KD, T, "w_lru_in", row=0))
            s.append(Product("lru_gates", 2 * KL, 1, T, "w_lru_gates", per_chunk=4, readers=["act"] * 2 * KL))
            s.append(Product("lru_gate", KL, KD, T, "w_lru_in", row=KL))
            s.append(Product("lru_out", KD, KL, T, "w_lru_out", cuts=LRU_CUTS))
        else:
            s.append(Product("mla_down", 6, KD, T, "w_mla_down"))
            s.append(Product("mla_uq", 12, 3, T, "w_mla_uq", per_chunk=2))
            s.append(Product("mla_ukv", 16, 2, T, "w_mla_ukv", per_chunk=4))
            s.append(Product("mla_out", KD, KD, T, "w_mla_o"))
        s.append(Product("ffn_in", 2 * KF, KD, T, "w_ffn_in", row=i * 2 * KF))
        s.append(Product("ffn_out", KD, KF, T, "w_ffn_out", row=i * KD, cuts=FF_CUTS))
    for i in range(DEPTH_2):
        s.append(Product("ada", 72, KD, 2, "w_ada", row=72 * i, split=False))
    for i in range(DEPTH_2):
        w = T2
        s.append(Product("ffn_in_2", 2 * KF, KD, w, "w_ffn_in_2", row=2 * i * 2 * KF, readers=GU_READERS))
        s.append(Product("ffn_out_2", KD, KF, w, "w_ffn_out_2", row=2 * i * KD, cuts=FF_CUTS))
        if i == 0:
            s.append(Product("att_in", 12, KD, T2, "w_att_in"))
            s.append(Product("att_out", KD, KD, T2, "w_att_out"))
        else:
            s.append(Product("ml_in", 25, KD, T2, "w_ml_in",
                             cols=[T2] + [T] * 4 + [T2] * 4 + [T2] * 8 + [T] * 8,
                             readers=["dve"] * 17 + ["act"] * 8))
            s.append(Product("ml_out", KD, KD, T, "w_ml_out"))
            w = T
        s.append(Product("ffn_in_2", 2 * KF, KD, w, "w_ffn_in_2", row=(2 * i + 1) * 2 * KF, readers=GU_READERS))
        s.append(Product("ffn_out_2", KD, KF, w, "w_ffn_out_2", row=(2 * i + 1) * KD, cuts=FF_CUTS))
    return s


class Tally:

    def __init__(self, engine, sem):
        self.engine, self.sem, self.n, self.i, self.per = engine, sem, 0, None, 0

    def at(self, n):
        return n if self.i is None else n + self.i * self.per

    def did(self, ins, by=1):
        ins.then_inc(self.sem, by)
        self.n += by
        return self.n

    def expect(self, by=1):
        self.n += by
        self.engine.wait_ge(self.sem, self.at(self.n))
        return self.n

    def need(self, n):
        if n > 0:
            self.engine.wait_ge(self.sem, self.at(n))

    def skip(self, n=1):
        self.n += n

    def link(self, ins):
        self.need(self.did(ins))

    def enter(self, i, per):
        self.i, self.per, self.start = i, per, self.n

    def leave(self, iterations):
        assert self.n - self.start == self.per, (self.n - self.start, self.per)
        self.n, self.i = self.start + self.per * iterations, None


def build_blocks(nc, dram, out):
    stages = plan()
    first_out, first_chunk, o, c = [], [], 0, 0
    for s in stages:
        first_out.append(o)
        first_chunk.append(c)
        o, c = o + (0 if not s.split else s.outs), c + s.n_chunks
    n_chunks = c
    owner, split_count = [], []
    n = 0
    for k, s in enumerate(stages):
        for j in range(s.n_chunks):
            n += s.split
            owner.append((k, j))
            split_count.append(n)
    freed, tally = [], {"dve": 0, "act": 0}
    for s in stages:
        if s.split:
            for e in s.readers:
                tally[e] += 1
                freed.append((e, tally[e]))

    done, parts = [], 0
    for c, (k, j) in enumerate(owner):
        s = stages[k]
        to, kk = s.tiles_of(j)[-1]
        if s.split and kk == s.ktiles - 1:
            done.append(("out", first_out[k] + to + 1))
        else:
            parts += 1
            done.append(("part", parts))

    def linear(value, at, step, i, iterations):
        v = value(at)
        if i is None:
            return v
        d = value(at + step) - v
        assert all(value(at + step * m) == v + d * m for m in range(iterations))
        return v + i * d if d else v

    def bodies(k, ahead=0):
        s = stages[k]
        per = 4 // s.per_chunk if s.per_chunk > 1 else 4 * len(s.cuts)
        plain = k > 0 and all(x.split and set(x.readers) == {"dve"} for x in stages[k - 1:k + 1])
        start = 0 if plain else 1
        n = 0
        if s.cols:
            return 0, 0, per
        while (start + n + 1) * 4 <= s.outs and (start + n + 1) * per + ahead <= s.n_chunks:
            n += 1
        return (start, n, per) if n >= 2 and per % SLOTS == 0 else (start, 0, per)

    ctx = ExitStack()
    with ctx:
        def sem(name):
            return ctx.enter_context(nc.semaphore(name))

        place = [nc.sbuf_base + (-nc.sbuf_base) % 32]

        def sb(name, shape, dt=F32, at=None):
            where = place if at is None else at
            t = nc.alloc_sbuf_tensor_at(name, shape, dt, offset=where[0])
            size = 4
            for x in shape[1:]:
                size *= x
            where[0] += size + (-size) % 32
            assert where[0] <= nc.sbuf_usable_end, (name, where[0], nc.sbuf_usable_end)
            return t

        raw = sb("raw", [P, SLOTS, CHUNK * P])
        w_hi = sb("w_hi", [P, SLOTS, CHUNK * P], F32R)
        w_lo = sb("w_lo", [P, SLOTS, CHUNK * P], F32R)
        res = sb("res", [P, KD, T2])
        x_hi = sb("x_hi", [P, KD, T2], F32R)
        x_lo = sb("x_lo", [P, KD, T2], F32R)
        scaled = sb("scaled", [P, 2, T])
        silu = sb("silu", [P, 2, T2])
        up = sb("up", [P, T])
        prod = sb("prod", [P, T2])
        acc = sb("acc", [P, T2])
        rstd = sb("rstd", [P, T2])
        par = sb("par", [P, N_PARAM])
        cst = sb("cst", [P, N_CONST])
        cond = sb("cond", [P, KD, 2])
        mod = sb("mod", [P, DEPTH_2, 72, 2])
        decay_c = sb("decay_c", [P, 6, KL])
        region = place[0]

        at = [region]
        h_hi = sb("h_hi", [P, KF, T2], F32R, at)
        h_lo = sb("h_lo", [P, KF, T2], F32R, at)

        at = [region]
        cv_c = sb("cv_c", [P, KD, T], F32, at)
        cv_x = sb("cv_x", [P, KD, T + 2], F32, at)
        cv_y = sb("cv_y", [P, KD, T], F32, at)
        cv_hi = sb("cv_hi", [P, KD, T], F32R, at)
        cv_lo = sb("cv_lo", [P, KD, T], F32R, at)

        at = [region]
        lr_pad = sb("lr_pad", [P, 2, T + 3], F32, at)
        lr_rec = sb("lr_rec", [P, KL, T], F32, at)
        lr_rec_hi = sb("lr_rec_hi", [P, KL, T], F32R, at)
        lr_rec_lo = sb("lr_rec_lo", [P, KL, T], F32R, at)
        lr_r = sb("lr_r", [P, KL, T], F32, at)
        lr_i = sb("lr_i", [P, KL, T], F32, at)
        lr_a = sb("lr_a", [P, KL, T], F32, at)
        lr_t = sb("lr_t", [P, KL, T], F32, at)
        lr_g = sb("lr_g", [P, KL, T], F32, at)
        lr_o_hi, lr_o_lo = lr_rec_hi, lr_rec_lo

        at = [region]
        ma_q = sb("ma_q", [P, 12, T], F32, at)
        ma_k = sb("ma_k", [P, 9, T], F32, at)
        ma_v = sb("ma_v", [P, HEADS, T], F32, at)
        ma_vt = sb("ma_vt", [P, 2, HEADS * P], F32, at)
        ma_o_hi = sb("ma_o_hi", [P, HEADS, T], F32R, at)
        ma_o_lo = sb("ma_o_lo", [P, HEADS, T], F32R, at)
        ma_const = sb("ma_const", [P, N_MLA_CONST], F32, at)
        ma_pos = sb("ma_pos", [P, T], I32, at)
        ma_cos = sb("ma_cos", [P, T], F32, at)
        ma_sin = sb("ma_sin", [P, T], F32, at)
        ma_ang = sb("ma_ang", [P, 3, T], F32, at)
        work = list(at)
        ma_x_hi = sb("ma_x_hi", [P, 5, T], F32R, at)
        ma_x_lo = sb("ma_x_lo", [P, 5, T], F32R, at)
        work_2 = list(at)
        ma_acc = sb("ma_acc", [P, 2, T], F32, at)
        ma_rs = sb("ma_rs", [P, 2, T], F32, at)
        after_mla = list(at)

        at = [region]
        ga_rope = sb("ga_rope", [P, 2, T], F32, at)
        ga_q = sb("ga_q", [P, HEADS, T2], F32, at)
        ga_k = sb("ga_k", [P, 2, T2], F32, at)
        ga_v = sb("ga_v", [P, 2, T2], F32, at)
        ga_vt = sb("ga_vt", [P, 4, 2 * P], F32, at)

        so_pt = sb("so_pt", [P, 2, 4, T], F32, work)
        hn_sq = sb("hn_sq", [P, 2, T2], F32, work_2)
        at = after_mla
        hn_rs = sb("hn_rs", [32, T2], F32, at)
        rp = sb("rp", [P, 2, T], F32, at)
        so_s = sb("so_s", [P, 2, T], F32, at)
        so_p = sb("so_p", [P, 2, T2], F32, at)
        so_m = sb("so_m", [P, 2, 4], F32, at)

        at = [region]
        ml_const = sb("ml_const", [P, N_ML_CONST], F32, at)
        ml_pad = sb("ml_pad", [P, 2, T + 2], F32, at)
        ml_cv = sb("ml_cv", [P, 2, 2, T], F32, at)
        ml_q = sb("ml_q", [P, 4, T], F32, at)
        ml_k = sb("ml_k", [P, 4, T2], F32, at)
        ml_vt = sb("ml_vt", [P, 4, D], F32, at)
        ml_og = sb("ml_og", [P, KD, T], F32, at)
        ml_row = sb("ml_row", [64, 5, T2], F32, at)
        ml_col = sb("ml_col", [P, 4, 64], F32, at)
        ml_den = sb("ml_den", [P, 2, T], F32, at)
        ml_msk = sb("ml_msk", [P, 3 * P], F32, at)
        shared = at[0]
        ml_v = sb("ml_v", [P, KD, T2], F32, at)
        at = [shared]
        ml_h = sb("ml_h", [P, KD, T], F32, at)
        ml_e = sb("ml_e", [P, 4, T], F32, at)
        ml_pt = sb("ml_pt", [P, 4, T], F32, at)

        ps = ctx.enter_context(nc.psum_tensor("ps", [P, 8, 512], F32))

        landed = [sem(f"weights_landed_{i}") for i in range(SLOTS)]
        hi_split = sem("hi_split")
        lo_split = sem("lo_split")
        part_used = sem("part_used")
        out_ready = sem("out_ready")
        read_dve = sem("read_dve")
        read_act = sem("read_act")
        operand_ready = sem("operand_ready")
        dve_step = sem("dve_step")
        act_step = sem("act_step")
        inputs_landed = sem("inputs_landed")
        region_free = sem("region_free")
        consts_landed = sem("consts_landed")
        silu_ready = sem("silu_ready")
        sums_ready = sem("sums_ready")
        stat_ready = sem("stat_ready")
        std_ready = sem("std_ready")
        act_ready = sem("act_ready")
        dve_ready = sem("dve_ready")
        pe_ready = sem("pe_ready")
        squares_ready = sem("squares_ready")
        squares_used = sem("squares_used")
        scores_ready = sem("scores_ready")
        max_ready = sem("max_ready")
        probs_ready = sem("probs_ready")
        probs_scaled = sem("probs_scaled")
        transposed = sem("transposed")
        turned = sem("turned")
        pv_done = sem("pv_done")
        head_squares = sem("head_squares")
        head_squares_used = sem("head_squares_used")
        for_act = sem("for_act")
        for_dve = sem("for_dve")
        result_ready = sem("result_ready")
        stored = sem("stored")

        def const(name, n=None, rows=P):
            a = CONST_AT[name]
            return cst[0:rows, a:a + (n or CONST_SIZES[name])]

        def param(name, i=0, rows=P):
            a = PARAM_AT[name] + i
            return par[0:rows, a:a + 1]

        ones = const("ones")

        OPERAND = dict(conv_out=(cv_hi, cv_lo, 0), lru_gates=(lr_rec_hi, lr_rec_lo, 0),
                       lru_out=(lr_o_hi, lr_o_lo, 0), mla_uq=(ma_x_hi, ma_x_lo, 0),
                       mla_ukv=(ma_x_hi, ma_x_lo, 3), mla_out=(ma_o_hi, ma_o_lo, 0),
                       ffn_out=(h_hi, h_lo, 0), ffn_out_2=(h_hi, h_lo, 0))
        FRESH = dict(conv_c=KD, conv_out=KD, lru_rec=KD, lru_gates=KL, lru_out=KL, mla_down=KD, mla_uq=3,
                     mla_ukv=2, mla_out=KD, ffn_in=KD, ffn_out=KF, ffn_in_2=KD, ffn_out_2=KF, att_in=KD,
                     att_out=2 * HEADS, ml_in=KD, ml_out=KD)

        def mla_norms():
            sel = [ma_const[0:32, P * n:P * n + P] for n in range(5)]
            one = [const("ident", rows=32)[:, r:r + 1].to_broadcast([32, P]) for r in range(16)]
            return ([(ma_q[:, h, :], h, False, param("qn_norm"), one[h]) for h in range(8)]
                    + [(ma_k[:, h, :], 8 + h, False, param("kn_norm"), one[8 + h]) for h in range(8)]
                    + [(ma_q[:, 8 + n, :], 16 + 2 * n, True, param("qr_norm"), sel[n]) for n in range(4)]
                    + [(ma_k[:, 8, :], 24, True, param("kr_norm"), sel[4])])

        def gqa_norms():
            one = [const("ident", rows=32)[:, r:r + 1].to_broadcast([32, P]) for r in range(16)]
            return ([(ga_q[:, h, :], h, False, param("att_q_gain"), one[h]) for h in range(8)]
                    + [(ga_k[:, h, :], 8 + h, False, param("att_k_gain"), one[8 + h]) for h in range(2)])

        mla_ropes = [(ma_q[:, 8 + n, :]) for n in range(4)] + [ma_k[:, 8, :]]
        gqa_ropes = [ga_q[:, h, 0:T] for h in range(8)] + [ga_k[:, h, 0:T] for h in range(2)]

        def mla_units():
            units = []
            for h in range(HEADS):
                half = slice(64 * (h % 2), 64 * (h % 2) + 64)
                for i in range(2):
                    rows, keys = slice(i * P, i * P + P), (i + 1) * P
                    mask = ma_const[:, 5 * P + (1 - i) * P:7 * P]
                    units.append(([(ma_q[:, h, rows], ma_k[:, h, 0:keys]),
                                   (ma_q[half, 8 + h // 2, rows], ma_k[half, 8, 0:keys])], keys, mask))
            return units

        def gqa_units():
            units = []
            for h in range(HEADS):
                for i in range(4):
                    keys = slice(0, T2) if i < 2 else slice(T, T2)
                    units.append(([(ga_q[:, h, i * P:i * P + P], ga_k[:, h // 4, keys])],
                                  T2 if i < 2 else T, None))
            return units

        def mla_groups():
            return [([(ma_vt[:, kt, h * P:h * P + P], kt, kt * P) for kt in range(2)],
                     ma_o_hi[:, h, :], ma_o_lo[:, h, :]) for h in range(HEADS)]

        def gqa_groups():
            groups = []
            for h in range(HEADS):
                v = slice((h // 4) * P, (h // 4) * P + P)
                groups.append(([(ga_vt[:, kt, v], kt, 0) for kt in range(4)],
                               x_hi[:, h, 0:T], x_lo[:, h, 0:T]))
                groups.append(([(ga_vt[:, 2 + kt, v], kt, 0) for kt in range(2)],
                               x_hi[:, h, T:T2], x_lo[:, h, T:T2]))
            return groups

        def lat_keys(direction):
            if direction == 0:
                return [(2, 0, T, None), (3, 0, T, None), (0, 0, T, 0), (1, P, P, 0)]
            return [(2, 0, T, None), (3, 0, T, None), (1, 0, T, P), (0, 0, P, 2 * P)]

        def ml_sq(h, v):
            n = 2 * h + v
            return ml_e[:, n, :] if n < 4 else ml_pt[:, n - 4, :]

        block = ctx.enter_context(nc.Block())

        @block.sync
        def _(sp):
            def small(dst, src):
                sp.dma_start(dst, src).then_inc(inputs_landed, 16)

            def load(k, j, i, iterations, per):
                s = stages[k]
                c = first_chunk[k] + j
                if c >= SLOTS:
                    before = c - SLOTS
                    if stages[owner[before][0]].split:
                        v = linear(lambda x: split_count[x], before, per, i, iterations)
                        sp.wait_ge(hi_split, v)
                        sp.wait_ge(lo_split, v)
                    else:
                        sp.wait_ge(part_used, linear(lambda x: done[x][1], before, per, i, iterations))
                tiles = s.tiles_of(j)
                if s.per_chunk > 1:
                    row, a = s.row + j, 0
                    step = per
                else:
                    row, a = s.row + tiles[0][0], tiles[0][1] * P
                    step = 4
                n = len(tiles) * P
                src = dram[s.weights][row if i is None else row + i * step, :, a:a + n]
                sp.dma_start(raw[:, c % SLOTS, 0:n], src).then_inc(landed[c % SLOTS], 16)

            small(par[:], dram["params"])
            small(cst[:], dram["consts"])
            small(res[:, :, 0:T], dram["x"])
            for k, s in enumerate(stages):
                start, count, per = bodies(k)
                j = 0
                if count:
                    for j in range(start * per):
                        load(k, j, None, 1, per)
                    with sp.Fori(0, count) as i:
                        for j in range(per):
                            load(k, start * per + j, i, count, per)
                    j = (start + count) * per
                for j in range(j, s.n_chunks):
                    load(k, j, None, 1, per)
            sp.wait_ge(result_ready, 1)
            sp.dma_start(out, res[:, :, 0:T]).then_inc(stored, 16)
            sp.wait_ge(stored, 16)

        @block.gpsimd
        def _(pool):
            pool.dma_start(res[:, :, T:T2], dram["ctx"]).then_inc(consts_landed, 16)
            pool.wait_ge(region_free, 1)
            pool.dma_start(ma_const[:], dram["mla_consts"]).then_inc(consts_landed, 16)
            pool.dma_start(ma_pos[:], dram["positions"].to_broadcast([P, T])).then_inc(consts_landed, 16)
            pool.wait_ge(region_free, 2)
            pool.dma_start(ga_rope[:], dram["gqa_rope"]).then_inc(consts_landed, 16)
            pool.wait_ge(region_free, 3)
            pool.dma_start(ml_const[:], dram["ml_consts"]).then_inc(consts_landed, 16)

        @block.tensor
        def _(pe):
            opnd = Tally(pe, operand_ready)
            sums = Tally(pe, sums_ready)
            stat = Tally(pe, stat_ready)
            from_dve = Tally(pe, dve_ready)
            from_act = Tally(pe, act_ready)
            mine = Tally(pe, pe_ready)
            sq_in, sq_out = Tally(pe, squares_ready), Tally(pe, squares_used)
            head_sq, head_sq_used = Tally(pe, head_squares), Tally(pe, head_squares_used)
            cnt = dict(u=0, g=0)

            def ones_sum(bank, src, width, last=True, start=True, stop=True):
                m = pe.matmul(ps[:, bank, 0:width], ones, src, start=start, stop=stop)
                if last:
                    stat.did(m)

            def output(k, o, i, iterations, per):
                s = stages[k]
                g = first_out[k] + o
                bank = g % BANKS
                hi, lo, base = OPERAND.get(s.name, (x_hi, x_lo, 0))
                width = s.cols[o] if s.cols else s.width
                dst = ps[:, bank, 0:width]
                if g >= BANKS:
                    who = freed[g - BANKS][0]
                    v = linear(lambda x: freed[x][1], g - BANKS, 4, i, iterations)
                    pe.wait_ge(read_dve if who == "dve" else read_act, v)
                for j in s.chunk_of(o):
                    c = first_chunk[k] + j
                    tiles = s.tiles_of(j)
                    v = linear(lambda x: split_count[x], c, per, i, iterations)
                    pe.wait_ge(hi_split, v)
                    pe.wait_ge(lo_split, v)
                    slot = c % SLOTS
                    for n, (to, kk) in enumerate(tiles):
                        if to != o:
                            continue
                        cols = slice(n * P, n * P + P)
                        x = kk + base if s.name != "lru_gates" else o // 2
                        xh, xl = hi[:, x, 0:width], lo[:, x, 0:width]
                        first, last = kk == 0, kk == s.ktiles - 1
                        pe.matmul(dst, w_hi[:, slot, cols], xh, start=first, stop=False)
                        pe.matmul(dst, w_hi[:, slot, cols], xl, start=False, stop=False)
                        m = pe.matmul(dst, w_lo[:, slot, cols], xh, start=False, stop=last)
                        if last:
                            m.then_inc(out_ready, 1)
                        elif n == len(tiles) - 1:
                            m.then_inc(part_used, 1)

            def run(k):
                s = stages[k]
                start, count, per = bodies(k)
                o = 0
                if count:
                    for o in range(start * 4):
                        output(k, o, None, 1, per)
                    with pe.Fori(0, count) as i:
                        for o in range(4):
                            output(k, start * 4 + o, i, count, per)
                    o = (start + count) * 4
                for o in range(o, s.outs):
                    output(k, o, None, 1, per)

            def ada(k):
                s = stages[k]
                layer = s.row // 72
                with pe.Fori(0, s.outs // SLOTS) as i:
                    for o in range(SLOTS):
                        c = first_chunk[k] + o
                        pe.wait_ge(landed[c % SLOTS], 16 * (c // SLOTS + 1) + i * 16)
                        for kk in range(KD):
                            m = pe.matmul(ps[:, 6 + layer, bass.ds(2 * o + i * 2 * SLOTS, 2)],
                                          raw[:, c % SLOTS, kk * P:kk * P + P],
                                          cond[:, kk, :], start=(kk == 0), stop=(kk == KD - 1))
                        m.then_inc(part_used, 1)

            def layer_norm_sums(width):
                sums.expect()
                ones_sum(4, acc[:, 0:width], width)
                for o in range(KD):
                    sq_in.expect()
                    sq_out.did(pe.matmul(ps[:, 5, 0:width], ones, silu[:, o % 2, 0:width],
                                         start=(o == 0), stop=(o == KD - 1)))

            def head_norms(tiles, width):
                for n, (x, row, halves, gain, one) in enumerate(tiles):
                    head_sq.expect()
                    z = CONST_AT["sel2" if halves else "sel"] + 31 - row
                    m = pe.matmul(ps[0:32, 4, 0:width], cst[:, z:z + 32], hn_sq[:, n % 2, 0:width],
                                  start=(n == 0), stop=(n == len(tiles) - 1))
                    (head_sq_used if n < len(tiles) - 1 else stat).did(m)
                from_dve.expect()
                for n, (x, row, halves, gain, one) in enumerate(tiles):
                    if n >= 2:
                        from_dve.expect()
                    mine.did(pe.matmul(ps[:, 5 + n % 2, 0:width], one, hn_rs[:, 0:width], start=True, stop=True))
                from_dve.expect(min(2, len(tiles)))

            def ropes(tiles):
                for n, x in enumerate(tiles):
                    if n >= 2:
                        from_dve.expect()
                    mine.did(pe.matmul(ps[:, 4 + n % 2, 0:T], const("rot"), x, start=True, stop=True))
                from_dve.expect(3)

            def transposes(source, n_tiles, tokens, heads):
                jobs = [(tt, h) for tt in range(tokens) for h in range(heads)]
                for n in range(0, len(jobs), 4):
                    if n >= 8:
                        from_act.expect()
                    for q, (tt, h) in enumerate(jobs[n:n + 4]):
                        m = pe.transpose(ps[:, 6 + (n // 4) % 2, q * P:q * P + P],
                                         source[:, h, tt * P:tt * P + P], const("ident"))
                    mine.did(m)
                from_act.expect(min(2, len(jobs) // 4))

            def attention(units, groups):
                u0, g0 = cnt["u"], cnt["g"]

                def scores(u):
                    parts, keys, _ = units[u]
                    if u >= 2:
                        pe.wait_ge(probs_ready, u0 + u - 1)
                    for n, (q, kx) in enumerate(parts):
                        m = pe.matmul(ps[:, 4 + u % 2, 0:keys], q, kx, start=(n == 0), stop=(n == len(parts) - 1))
                    m.then_inc(scores_ready, 1)

                def turn(u):
                    keys = units[u][1]
                    pe.wait_ge(probs_scaled, u0 + u + 1)
                    if u >= 2:
                        pe.wait_ge(turned, u0 + u - 1)
                    for kt in range(keys // P):
                        m = pe.transpose(ps[:, 6 + u % 2, kt * P:kt * P + P], so_p[:, u % 2, kt * P:kt * P + P],
                                         const("ident"))
                    m.then_inc(transposed, 1)

                def values(g):
                    pe.wait_ge(turned, u0 + 2 * g + 2)
                    if g >= 2:
                        pe.wait_ge(operand_ready, opnd.n + g - 1)
                    parts = groups[g][0]
                    for n, (v, kt, a) in enumerate(parts):
                        m = pe.matmul(ps[:, g % 2, a:T], v, so_pt[:, g % 2, kt, a:T], start=(n == 0),
                                      stop=(n == len(parts) - 1), skip_group_check=True)
                    m.then_inc(pv_done, 1)

                scores(0)
                for u in range(len(units)):
                    if u + 1 < len(units):
                        scores(u + 1)
                    if u % 2 == 0 and u >= 2:
                        values(u // 2 - 1)
                    turn(u)
                values(len(groups) - 1)
                cnt["u"] += len(units)
                cnt["g"] += len(groups)

            def mlstm():
                from_dve.expect()
                for t in range(4):
                    m = pe.transpose(ps[:, 4, 64 * t:64 * t + 64], ml_row[:, 2, t * P:t * P + P],
                                     const("ident", rows=64)[:, 0:64])
                mine.did(m)
                for h in range(4):
                    if h:
                        from_dve.expect()
                    for t in range(4):
                        m = pe.matmul(ps[:, t // 2, (t % 2) * T:(t % 2) * T + T], ml_k[:, h, t * P:t * P + P],
                                      ml_q[:, h, :], start=True, stop=True)
                    mine.did(m)
                    for d in range(2):
                        from_dve.expect()
                        row = const("ident", rows=64)[:, 32 * d + h:32 * d + h + 1].to_broadcast([64, P])
                        pe.matmul(ps[:, 4, 0:T], row, ml_row[:, 3, 0:T], start=True, stop=True)
                        mine.did(pe.matmul(ps[:, 4, T:T2], row, ml_row[:, 4, 0:T], start=True, stop=True))
                        from_dve.expect()
                        for vt in range(2):
                            for n, (t, a, w, _) in enumerate(lat_keys(d)):
                                pe.matmul(ps[:, 5, vt * T + a:vt * T + a + w],
                                          ml_vt[:, t, (2 * h + vt) * P:(2 * h + vt) * P + P],
                                          ml_pt[:, n, 0:w], start=(n == 0), stop=(n == 3), skip_group_check=True)
                        for n, (t, a, w, _) in enumerate(lat_keys(d)):
                            m = pe.matmul(ps[:, 6, a:a + w], ones, ml_pt[:, n, 0:w], start=(n == 0), stop=(n == 3),
                                          skip_group_check=True)
                        mine.did(m)
                for h in range(4):
                    from_dve.expect()
                    for v in range(2):
                        m = pe.matmul(ps[:, h, 0:T], ones, ml_h[:, 2 * h + v, :], start=(v == 0), stop=(v == 1))
                    mine.did(m)
                for h in range(4):
                    from_act.expect()
                    for v in range(2):
                        m = pe.matmul(ps[:, 4 + h, 0:T], ones, ml_sq(h, v), start=(v == 0),
                                      stop=(v == 1))
                    mine.did(m)

            pe.wait_ge(inputs_landed, 48)
            from_act.expect()
            for k, s in enumerate(stages):
                if s.name in ("conv_c", "lru_rec", "mla_down", "ffn_in"):
                    opnd.expect(FRESH[s.name])
                    sums.expect()
                    ones_sum(4, acc[:, 0:T], T)
                elif s.name == "mla_uq":
                    opnd.expect(5)
                    for n in range(2):
                        sums.expect()
                        ones_sum(4 + n, ma_acc[:, n, :], T)
                elif s.name == "mla_ukv":
                    pass
                elif s.name in FRESH:
                    opnd.expect(FRESH[s.name])
                if s.name == "ada":
                    ada(k)
                else:
                    run(k)
                if s.name == "mla_ukv":
                    pe.wait_ge(read_dve, freed[first_out[k] + 15][1])
                    transposes(ma_v, HEADS, 2, HEADS)
                    head_norms(mla_norms(), T)
                    ropes(mla_ropes)
                    attention(mla_units(), mla_groups())
                elif s.name == "att_in":
                    pe.wait_ge(read_dve, freed[first_out[k] + 11][1])
                    transposes(ga_v, 2, 4, 2)
                    head_norms(gqa_norms(), T2)
                    ropes(gqa_ropes)
                    attention(gqa_units(), gqa_groups())
                elif s.name == "ml_in":
                    pe.wait_ge(read_dve, freed[first_out[k] + 16][1])
                    transposes(ml_v, KD, 4, KD)
                    mlstm()
                elif s.name in ("ffn_out_2", "att_out", "ml_out"):
                    layer_norm_sums(s.width)

        @block.vector
        def _(dve):
            step = Tally(dve, dve_step)
            opnd = Tally(dve, operand_ready)
            sums = Tally(dve, sums_ready)
            stat = Tally(dve, stat_ready)
            std = Tally(dve, std_ready)
            silus = Tally(dve, silu_ready)
            to_pe, from_pe = Tally(dve, dve_ready), Tally(dve, pe_ready)
            to_act, from_act = Tally(dve, for_act), Tally(dve, for_dve)
            head_sq, head_sq_used = Tally(dve, head_squares), Tally(dve, head_squares_used)
            region_done = Tally(dve, region_free)
            tallies = dict(step=step, opnd=opnd, silus=silus)
            link = step.link
            cnt = dict(u=0, g=0)
            split_to = [0]
            tt, ts, stt = dve.tensor_tensor, dve.tensor_scalar, dve.scalar_tensor_tensor

            def split(c, i=None, iterations=1, per=0):
                k, j = owner[c]
                n = len(stages[k].tiles_of(j)) * P
                slot = c % SLOTS
                dve.wait_ge(hi_split, linear(lambda x: split_count[x], c, per, i, iterations))
                tt(w_lo[:, slot, 0:n], raw[:, slot, 0:n], w_hi[:, slot, 0:n].bitcast(F32),
                   ALU.subtract).then_inc(lo_split, 1)

            def split_ahead(k, o):
                last = min(first_chunk[k] + stages[k].chunk_of(o)[-1] + AHEAD, n_chunks - 1)
                while split_to[0] <= last:
                    if stages[owner[split_to[0]][0]].split:
                        split(split_to[0])
                    split_to[0] += 1

            def arrived(k, o, i=None, iterations=1):
                g = first_out[k] + o
                dve.wait_ge(out_ready, linear(lambda x: x + 1, g, 4, i, iterations))
                s = stages[k]
                return ps[:, g % BANKS, 0:(s.cols[o] if s.cols else s.width)]

            def bank_read(k, o, ins, i=None, iterations=1):
                g = first_out[k] + o
                ins.then_inc(read_dve, 1)
                dve.wait_ge(read_dve, linear(lambda x: freed[x][1], g, 4, i, iterations))

            def next_operand(o, gain):
                link(ts(up[:], res[:, o, 0:T], gain, None, ALU.mult))
                link(dve.tensor_copy(x_hi[:, o, 0:T], up[:]))
                opnd.did(tt(x_lo[:, o, 0:T], up[:], x_hi[:, o, 0:T].bitcast(F32), ALU.subtract))
                if o == 0:
                    link(tt(acc[:, 0:T], res[:, o, 0:T], res[:, o, 0:T], ALU.mult))
                    return
                link(tt(prod[:, 0:T], res[:, o, 0:T], res[:, o, 0:T], ALU.mult))
                ins = tt(acc[:, 0:T], acc[:, 0:T], prod[:, 0:T], ALU.add)
                if o == KD - 1:
                    sums.did(ins)
                else:
                    link(ins)

            def inverse_rms():
                std.expect()
                link(dve.reciprocal(rstd[:, 0:T], rstd[:, 0:T]))

            def to_operand(hi, lo, src):
                link(dve.tensor_copy(hi, src))
                opnd.did(tt(lo, src, hi.bitcast(F32), ALU.subtract))

            def conv(dst, src, taps, width, bias=None, last=None):
                n = len(taps)
                for m, j in enumerate(reversed(range(n))):
                    if m == 0:
                        if bias is None:
                            ins = ts(dst, src(j), taps[j], None, ALU.mult)
                        else:
                            ins = ts(dst, src(j), taps[j], bias, ALU.mult, ALU.add)
                    else:
                        ins = stt(dst, src(j), taps[j], dst, ALU.mult, ALU.add)
                    (last if last and m == n - 1 else link)(ins)

            def read_out(k, o, layer, i=None, iterations=1):
                s = stages[k]
                name = s.name
                bank = arrived(k, o, i, iterations)
                done_with = lambda ins: bank_read(k, o, ins, i, iterations)
                r = rstd[:, 0:T]
                if name == "conv_c":
                    done_with(tt(cv_c[:, o, :], bank, r, ALU.mult))
                elif name == "conv_h":
                    done_with(tt(up[:], bank, r, ALU.mult))
                    link(tt(cv_x[:, o, 2:], up[:], cv_c[:, o, :], ALU.mult))
                    taps = [param("conv_w", ((layer // 3) * KD + o) * 3 + j) for j in range(3)]
                    conv(cv_y[:, o, :], lambda j: cv_x[:, o, j:j + T], taps, T)
                elif name == "conv_b":
                    done_with(tt(up[:], bank, r, ALU.mult))
                    link(tt(prod[:, 0:T], up[:], cv_y[:, o, :], ALU.mult))
                    to_operand(cv_hi[:, o, :], cv_lo[:, o, :], prod[:, 0:T])
                elif name == "lru_rec":
                    pad = lr_pad[:, o % 2, :]
                    done_with(tt(pad[:, 3:], bank, r, ALU.mult))
                    taps = [param("lru_conv_w", o * 4 + j) for j in range(4)]
                    conv(lr_rec[:, o, :], lambda j: pad[:, j:j + T], taps, T, bias=param("lru_conv_b", o))
                    to_operand(lr_rec_hi[:, o, :], lr_rec_lo[:, o, :], lr_rec[:, o, :])
                elif name == "lru_gate":
                    done_with(tt(lr_g[:, o, :], bank, r, ALU.mult))
                    from_act.expect()
                    link(tt(lr_t[:, o, :], lr_t[:, o, :], lr_i[:, o, :], ALU.mult))
                    link(tt(lr_t[:, o, :], lr_t[:, o, :], lr_rec[:, o, :], ALU.mult))
                    link(dve.tensor_tensor_scan(lr_r[:, o, :], lr_a[:, o, :], lr_t[:, o, :], 0.0, ALU.mult, ALU.add))
                elif name == "mla_down":
                    if o == 5:
                        done_with(tt(ma_k[:, 8, :], bank, r, ALU.mult))
                        return
                    done_with(tt(up[:], bank, r, ALU.mult))
                    n, first = (0, 0) if o < 3 else (1, 3)
                    if o == first:
                        link(tt(ma_acc[:, n, :], up[:], up[:], ALU.mult))
                    else:
                        link(tt(prod[:, 0:T], up[:], up[:], ALU.mult))
                        (sums.did if o in (2, 4) else link)(
                            tt(ma_acc[:, n, :], ma_acc[:, n, :], prod[:, 0:T], ALU.add))
                    gain = param("q_norm", o) if o < 3 else param("kv_norm", o - 3)
                    link(ts(scaled[:, 0, :], up[:], gain, None, ALU.mult))
                    to_operand(ma_x_hi[:, o, :], ma_x_lo[:, o, :], scaled[:, 0, :])
                elif name == "mla_uq":
                    done_with(tt(ma_q[:, o, :], bank, ma_rs[:, 0, :], ALU.mult))
                elif name == "mla_ukv":
                    dst = ma_k[:, o, :] if o < 8 else ma_v[:, o - 8, :]
                    done_with(tt(dst, bank, ma_rs[:, 1, :], ALU.mult))
                elif name == "ffn_in":
                    n = o // 2
                    if o % 2 == 0:
                        done_with(tt(scaled[:, n % 2, :], bank, r, ALU.mult))
                        return
                    done_with(tt(up[:], bank, r, ALU.mult))
                    silus.expect()
                    link(tt(prod[:, 0:T], up[:], silu[:, n % 2, 0:T], ALU.mult))
                    t = n if i is None else n + i * 2
                    to_operand(h_hi[:, t, 0:T], h_lo[:, t, 0:T], prod[:, 0:T])
                elif name == "ffn_in_2":
                    n, w = o // 2, s.width
                    g = first_out[k] + o - 1
                    dve.wait_ge(read_act, linear(lambda x: freed[x][1], g, 4, i, iterations))
                    opnd.need(opnd.n)
                    done_with(tt(prod[:, 0:w], bank, silu[:, n % 2, 0:w], ALU.mult))
                    t = n if i is None else n + i * 2
                    to_operand(h_hi[:, t, 0:w], h_lo[:, t, 0:w], prod[:, 0:w])
                elif name in ("conv_out", "lru_out", "mla_out", "ffn_out"):
                    done_with(tt(res[:, o, 0:T], bank, res[:, o, 0:T], ALU.add))
                    if name != "ffn_out":
                        next_operand(o, param("ffn_norm", layer * KD + o))
                    elif layer + 1 < DEPTH:
                        next_operand(o, param("mix_norm", (layer + 1) * KD + o))
                elif name == "att_in":
                    dst = ga_q[:, o, :] if o < 8 else ga_k[:, o - 8, :] if o < 10 else ga_v[:, o - 10, :]
                    done_with(dve.tensor_copy(dst, bank))
                elif name == "ml_in":
                    if o == 0:
                        link(ts(ml_row[:, 0, :], bank[0:64, :], param("ml_bias_i", rows=64), None, ALU.add))
                        done_with(dve.tensor_copy(ml_row[:, 1, :], bank[64:P, :]))
                        link(ts(ml_row[:, 1, :], ml_row[:, 1, :], param("ml_bias_f", rows=64), None, ALU.add))
                    elif o < 9:
                        taps = [param("ml_conv_w", (o - 1) * 3 + j) for j in range(3)]
                        if o >= 3:
                            from_act.expect()
                        if o < 5:
                            done_with(dve.tensor_copy(ml_pad[:, 0, 1:T + 1], bank))
                            conv(ml_cv[:, o % 2, 0, :], lambda j: ml_pad[:, 0, j:j + T], taps, T,
                                 bias=param("ml_conv_b", o - 1), last=to_act.did)
                        else:
                            done_with(dve.tensor_copy(ml_pad[:, :, 1:T + 1], bank.rearrange("p (a t) -> p a t", a=2)))
                            conv(ml_cv[:, o % 2, :, :], lambda j: ml_pad[:, :, j:j + T], taps, T2,
                                 bias=param("ml_conv_b", o - 1), last=to_act.did)
                    else:
                        done_with(dve.tensor_copy(ml_v[:, o - 9, :], bank))

            def halves(width):
                return [(0, T, 0)] + ([(T, T2, 1)] if width == T2 else [])

            def delta(k, o, layer, pos):
                s = stages[k]
                bank = arrived(k, o)
                w = s.width
                hs = halves(w)
                for a, b, v in hs:
                    gate = mod[:, layer, (2 + 3 * pos) * KD + o, v:v + 1]
                    ins = ts(prod[:, a:b], bank[:, a:b], gate, None, ALU.mult)
                    if b == w:
                        bank_read(k, o, ins)
                    else:
                        step.did(ins)
                link(stt(res[:, o, 0:w], res[:, o, 0:w], ALPHA, prod[:, 0:w], ALU.mult, ALU.add))
                if o == 0:
                    link(dve.tensor_copy(acc[:, 0:w], res[:, o, 0:w]))
                else:
                    ins = tt(acc[:, 0:w], acc[:, 0:w], res[:, o, 0:w], ALU.add)
                    (sums.did if o == KD - 1 else link)(ins)

            def modulated(o, layer, pos, width):
                for a, b, v in halves(width):
                    shift = mod[:, layer, 3 * pos * KD + o, v:v + 1]
                    scale = mod[:, layer, (3 * pos + 1) * KD + o, v:v + 1]
                    link(ts(prod[:, a:b], res[:, o, a:b], scale, shift, ALU.mult, ALU.add))
                to_operand(x_hi[:, o, 0:width], x_lo[:, o, 0:width], prod[:, 0:width])
                opnd.need(opnd.n)

            def post_norm(layer, pos, w):
                stat.expect()
                link(ts(prod[:, 0:w], ps[:, 4, 0:w], 1.0 / D, None, ALU.mult))
                for o in range(KD):
                    to_act.did(tt(res[:, o, 0:w], res[:, o, 0:w], prod[:, 0:w], ALU.subtract))
                std.expect()
                link(dve.reciprocal(rstd[:, 0:w], rstd[:, 0:w]))
                for o in range(KD):
                    n = (layer * 3 + pos) * KD + o
                    link(tt(res[:, o, 0:w], res[:, o, 0:w], rstd[:, 0:w], ALU.mult))
                    ins = ts(res[:, o, 0:w], res[:, o, 0:w], param("ln_g", n), param("ln_b", n), ALU.mult, ALU.add)
                    if layer == DEPTH_2 - 1 and pos == 2:
                        if o == KD - 1:
                            ins.then_inc(result_ready, 1)
                        continue
                    link(ins)
                    modulated(o, layer + (pos == 2), (pos + 1) % 3, w)

            def log_sigmoid(x, t, n):
                link(stt(t[0], x, -1.0, x, ALU.mult, ALU.max))
                to_act.did(ts(t[0], t[0], -1.0, None, ALU.mult))
                from_act.expect()
                to_act.did(ts(t[2], t[1], 1.0, None, ALU.add))
                from_act.expect()
                link(stt(t[1], t[2], -1.0, t[1], ALU.add, ALU.subtract))
                link(dve.reciprocal(t[2], t[2]))
                link(tt(t[1], t[1], t[2], ALU.mult))
                link(tt(t[0], t[0], t[1], ALU.subtract))
                link(stt(x, x, 0.0, t[0], ALU.min, ALU.subtract))

            def rope_tables():
                ang, turns, r = ma_ang[:, 0, :], ma_ang[:, 1, :], ma_ang[:, 2, :]
                link(dve.tensor_copy(r, ma_pos[:]))
                link(ts(ang, r, const("inv_freq"), None, ALU.mult))
                magic = 1.5 * 2.0 ** 23
                link(ts(turns, ang, 1.0 / (2 * math.pi), None, ALU.mult))
                link(ts(turns, turns, magic, None, ALU.add))
                link(ts(turns, turns, magic, None, ALU.subtract))
                c1, c2 = 6.28125, 0.0019350051879882812
                for part in (c1, c2, 2 * math.pi - c1 - c2):
                    link(stt(ang, turns, -part, ang, ALU.mult, ALU.add))
                link(ts(ang, ang, math.pi, -math.pi, ALU.min, ALU.max))
                link(stt(r, ang, -1.0, ang, ALU.mult, ALU.max))
                to_act.did(ts(r, r, -1.0, math.pi / 2, ALU.mult, ALU.add))
                from_act.expect()

            def head_norms(tiles, width):
                base = head_sq_used.n
                for n, (x, row, pair, gain, one) in enumerate(tiles):
                    if n >= 2:
                        head_sq_used.need(base + n - 1)
                    head_sq.did(tt(hn_sq[:, n % 2, 0:width], x, x, ALU.mult))
                head_sq_used.skip(len(tiles) - 1)
                std.expect()
                to_pe.did(dve.reciprocal(hn_rs[:, 0:width], hn_rs[:, 0:width]))
                for n, (x, row, pair, gain, one) in enumerate(tiles):
                    from_pe.expect()
                    to_pe.did(stt(x, x, gain, ps[:, 5 + n % 2, 0:width], ALU.mult, ALU.mult))

            def ropes(tiles, cos, sin):
                for n, x in enumerate(tiles):
                    step.did(tt(rp[:, 0, :], x, cos, ALU.mult))
                    from_pe.expect()
                    to_pe.did(tt(rp[:, 1, :], ps[:, 4 + n % 2, 0:T], sin, ALU.mult))
                    to_pe.need(to_pe.n)
                    step.need(step.n)
                    ins = tt(x, rp[:, 0, :], rp[:, 1, :], ALU.add)
                    (to_pe.did if n == len(tiles) - 1 else link)(ins)

            def attention(units, groups, scale, masked):
                u0, g0 = cnt["u"], cnt["g"]

                def maximum(u):
                    keys, mask = units[u][1], units[u][2]
                    m = so_m[:, u % 2, :]
                    dve.wait_ge(scores_ready, u0 + u + 1)
                    src = ps[:, 4 + u % 2, 0:keys]
                    if u >= 2:
                        dve.wait_ge(probs_ready, u0 + u - 1)
                    if masked:
                        link(stt(so_s[:, u % 2, 0:keys], src, scale, mask, ALU.mult, ALU.add))
                        dve.tensor_reduce(m[:, 0:1], so_s[:, u % 2, 0:keys], AX.X, ALU.max,
                                          negate=True).then_inc(max_ready, 1)
                    else:
                        link(dve.tensor_reduce(m[:, 1:2], src, AX.X, ALU.max, negate=True))
                        ts(m[:, 0:1], m[:, 1:2], scale, None, ALU.mult).then_inc(max_ready, 1)

                def normalise(u):
                    keys = units[u][1]
                    dve.wait_ge(probs_ready, u0 + u + 1)
                    link(dve.reciprocal(so_m[:, u % 2, 3:4], so_m[:, u % 2, 2:3]))
                    p = so_p[:, u % 2, 0:keys]
                    ts(p, p, so_m[:, u % 2, 3:4], None, ALU.mult).then_inc(probs_scaled, 1)

                def result(g):
                    dve.wait_ge(pv_done, g0 + g + 1)
                    to_operand(groups[g][1], groups[g][2], ps[:, g % 2, 0:T])

                maximum(0)
                for u in range(len(units)):
                    if u + 1 < len(units):
                        maximum(u + 1)
                    if u % 2 == 1 and u >= 3:
                        result(u // 2 - 1)
                    normalise(u)
                result(len(groups) - 1)
                cnt["u"] += len(units)
                cnt["g"] += len(groups)

            def mlstm():
                for _ in range(2):
                    from_act.expect()
                link(ts(ml_q[:], ml_q[:], P ** -0.5, None, ALU.mult))
                r = [ml_row[:, n, :] for n in range(5)]
                log_sigmoid(r[1], [r[2], r[3], r[4]], T2)
                link(dve.memset(r[3], 1.0))

                def scan(dst, src, initial, op):
                    for lo, rev in ((0, False), (32, True)):
                        rows = slice(lo, lo + 32)
                        first = initial
                        for a in (T, 0):
                            d, s_, one = dst[rows, a:a + T], src[rows, a:a + T], r[3][rows, a:a + T]
                            if rev:
                                d, s_, one = d[:, ::-1], s_[:, ::-1], one[:, ::-1]
                            link(dve.tensor_tensor_scan(d, one, s_, first, ALU.mult, op))
                            end = a if rev else a + T - 1
                            first = dst[rows, end:end + 1]

                scan(r[4], r[1], 0.0, ALU.add)
                to_pe.did(tt(r[2], r[0], r[4], ALU.subtract))
                to_pe.need(to_pe.n)
                scan(r[1], r[2], 0.0, ALU.max)
                to_act.did(tt(r[4][:, 0:T], r[4][:, 0:T], r[1][:, 0:T], ALU.add))
                from_act.expect()
                from_pe.skip(len_transposes(4 * KD))
                from_pe.expect()
                link(dve.tensor_copy(ml_col[:], ps[:, 4, 0:T].rearrange("p (t r) -> p t r", t=4)))
                to_pe.did(dve.tensor_copy(r[3][:, 0:T], r[1][:, 0:T]))
                for h in range(4):
                    from_pe.expect()
                    for d in range(2):
                        from_pe.expect()
                        keys = lat_keys(d)
                        n = 0
                        for t, a, w, m in keys[2:]:
                            ins = tt(ml_msk[:, n:n + w], ps[:, 4, a:a + w], ml_const[:, m:m + w], ALU.add)
                            (to_act.did if n else step.did)(ins)
                            n += w
                        from_act.expect()
                        for n, (t, a, w, _) in enumerate(keys):
                            at_ = (t % 2) * T + a
                            ins = tt(ml_pt[:, n, 0:w], ps[:, t // 2, at_:at_ + w], ml_e[:, n, 0:w], ALU.mult)
                            (to_pe.did if n == 3 else step.did)(ins)
                        from_pe.expect()
                        den, inv = ml_den[:, 0, :], ml_den[:, 1, :]
                        link(dve.tensor_copy(den, ps[:, 6, 0:T]))
                        link(stt(inv, den, -1.0, den, ALU.mult, ALU.max))
                        link(tt(inv, inv, ps[:, 4, T:T2], ALU.max))
                        link(dve.reciprocal(inv, inv))
                        by = 1 if d == 0 else 2 if h < 3 else 4
                        for v in range(2):
                            dst, src = ml_h[:, 2 * h + v, :], ps[:, 5, v * T:v * T + T]
                            if d == 0:
                                ins = tt(dst, src, inv, ALU.mult)
                            else:
                                link(tt(den, src, inv, ALU.mult))
                                ins = tt(dst, dst, den, ALU.add)
                            if v == 1:
                                to_pe.did(ins, by)
                                to_pe.need(to_pe.n)
                            else:
                                link(ins)
                for h in range(4):
                    from_pe.expect()
                    link(ts(ml_den[:, 0, :], ps[:, h, 0:T], 1.0 / (2 * P), None, ALU.mult))
                    for v in range(2):
                        x = ml_h[:, 2 * h + v, :]
                        ins = tt(x, x, ml_den[:, 0, :], ALU.subtract)
                        (to_act.did if v else step.did)(ins)
                    to_act.need(to_act.n)
                from_pe.skip(4)
                for h in range(4):
                    from_act.expect()
                    link(dve.reciprocal(ml_q[:, h, :], ml_q[:, h, :]))
                    for v in range(2):
                        n = 2 * h + v
                        x = ml_h[:, n, :]
                        link(tt(x, x, ml_q[:, h, :], ALU.mult))
                        link(stt(x, x, param("ml_norm_g", n), ml_og[:, n, :], ALU.mult, ALU.mult))
                        to_operand(x_hi[:, n, 0:T], x_lo[:, n, 0:T], x)

            def run(k, layer, pos):
                s = stages[k]
                count = sum(bodies(k, AHEAD)[:2]) if s.name in ("ffn_in", "ffn_in_2") else 0
                def one(o, i=None, iterations=1):
                    if s.readers[o] == "act":
                        return
                    if s.name in ("ffn_out_2", "att_out", "ml_out"):
                        delta(k, o, layer, pos)
                    else:
                        read_out(k, o, layer, i, iterations)
                o = 0
                if count:
                    split_ahead(k, 0)
                    assert split_to[0] == first_chunk[k] + AHEAD + 1
                    one(0)
                    split_ahead(k, 1)
                    one(1)
                    split_ahead(k, 2)
                    one(2)
                    split_ahead(k, 3)
                    one(3)
                    counts = dict(step=4, opnd=2, silus=2) if s.name == "ffn_in" else dict(step=2, opnd=2, silus=0)
                    with dve.Fori(0, count - 1) as i:
                        for name, t in tallies.items():
                            t.enter(i, counts[name])
                        for o in range(4, 8):
                            split(first_chunk[k] + o + AHEAD, i, count - 1, 4)
                            one(o, i, count - 1)
                        for t in tallies.values():
                            t.leave(count - 1)
                    split_to[0] += 4 * (count - 1)
                    o = 4 * count
                for o in range(o, s.outs):
                    split_ahead(k, o)
                    one(o)

            def len_transposes(n):
                return n // 4

            dve.wait_ge(inputs_landed, 48)
            lam = decay_c[:, 3, :]
            link(dve.tensor_copy(lam, par[:, PARAM_AT["lam"]:PARAM_AT["lam"] + KL]))
            log_sigmoid(lam, [decay_c[:, n, :] for n in range(3)], KL)
            link(ts(decay_c[:, 4, :], lam, 8.0, None, ALU.mult))
            to_act.did(ts(decay_c[:, 5, :], lam, -8.0, None, ALU.mult))
            for o in range(KD):
                next_operand(o, param("mix_norm", o))
            layer, pos = 0, 0
            for k, s in enumerate(stages):
                name = s.name
                if name == "ada":
                    if s.row == 72:
                        dve.wait_ge(part_used, done[first_chunk[k] + s.n_chunks - 1][1])
                        for m in range(DEPTH_2):
                            a = PARAM_AT["ada_b"] + 72 * m
                            link(tt(mod[:, m], ps[:, 6 + m, 0:144].rearrange("p (n v) -> p n v", v=2),
                                    par[:, a:a + 72].unsqueeze(2).to_broadcast([P, 72, 2]), ALU.add))
                            for q in range(3):
                                x = mod[:, m, (3 * q + 1) * KD:(3 * q + 2) * KD, :]
                                link(ts(x, x, 1.0, None, ALU.add))
                                if q != 1:
                                    x = mod[:, m, (3 * q + 2) * KD:(3 * q + 3) * KD, :]
                                    link(ts(x, x, 0.5, None, ALU.mult))
                        dve.wait_ge(consts_landed, 48)
                        for o in range(KD):
                            modulated(o, 0, 0, T2)
                        layer, pos = 0, 0
                    continue
                if name in ("conv_c", "lru_rec", "mla_down", "ffn_in"):
                    stat.skip()
                    inverse_rms()
                if name == "conv_c":
                    link(dve.memset(cv_x[:, :, 0:2], 0.0))
                elif name == "lru_rec":
                    link(dve.memset(lr_pad[:, :, 0:3], 0.0))
                elif name == "lru_gate":
                    for n in range(KL):
                        from_act.expect()
                        link(tt(prod[:, 0:T], lr_a[:, n, :], lr_a[:, n, :], ALU.mult))
                        to_act.did(stt(lr_t[:, n, :], prod[:, 0:T], 1.0, lr_t[:, n, :], ALU.add, ALU.mult))
                        to_act.need(to_act.n)
                elif name == "mla_down":
                    region_done.did(dve.memset(ma_ang[:, 0, 0:1], 0.0))
                    region_done.need(region_done.n)
                elif name == "mla_uq":
                    stat.skip(2)
                    for n in range(2):
                        std.expect()
                        link(dve.reciprocal(ma_rs[:, n, :], ma_rs[:, n, :]))
                    dve.wait_ge(consts_landed, 48)
                    rope_tables()
                elif name == "att_in":
                    region_done.did(dve.memset(hn_rs[:, 0:1], 0.0))
                    region_done.need(region_done.n)
                elif name == "ml_in":
                    region_done.did(dve.memset(ml_pad[:], 0.0))
                    region_done.need(region_done.n)
                run(k, layer, pos)
                if name == "lru_gate":
                    for n in range(KL):
                        from_act.expect()
                        link(tt(prod[:, 0:T], lr_g[:, n, :], lr_r[:, n, :], ALU.mult))
                        to_operand(lr_o_hi[:, n, :], lr_o_lo[:, n, :], prod[:, 0:T])
                        opnd.need(opnd.n)
                elif name == "mla_ukv":
                    from_pe.skip(len_transposes(2 * HEADS))
                    stat.skip()
                    head_norms(mla_norms(), T)
                    ropes(mla_ropes, ma_cos[:], ma_sin[:])
                    attention(mla_units(), mla_groups(), (NOPE + ROPE) ** -0.5, True)
                elif name == "att_in":
                    from_pe.skip(len_transposes(8))
                    stat.skip()
                    head_norms(gqa_norms(), T2)
                    dve.wait_ge(consts_landed, 64)
                    ropes(gqa_ropes, ga_rope[:, 0, :], ga_rope[:, 1, :])
                    attention(gqa_units(), gqa_groups(), P ** -0.5, False)
                elif name == "ml_in":
                    dve.wait_ge(consts_landed, 80)
                    mlstm()
                elif name == "ffn_out":
                    layer += 1
                elif name in ("ffn_out_2", "att_out", "ml_out"):
                    post_norm(layer, pos, s.width)
                    layer, pos = (layer + 1, 0) if pos == 2 else (layer, pos + 1)

        @block.scalar
        def _(act):
            step = Tally(act, act_step)
            stat = Tally(act, stat_ready)
            std = Tally(act, std_ready)
            silus = Tally(act, silu_ready)
            to_pe, from_pe = Tally(act, act_ready), Tally(act, pe_ready)
            from_dve, to_dve = Tally(act, for_act), Tally(act, for_dve)
            sq, sq_used = Tally(act, squares_ready), Tally(act, squares_used)
            tallies = dict(silus=silus)
            cnt = dict(u=0, g=0)
            split_to = [0]
            f = act.activation

            def split(c, i=None, iterations=1, per=0):
                k, j = owner[c]
                n = len(stages[k].tiles_of(j)) * P
                slot = c % SLOTS
                v = 16 * (c // SLOTS + 1)
                act.wait_ge(landed[slot], v if i is None else v + i * (16 * (per // SLOTS)))
                before = c - SLOTS
                while before >= 0 and not stages[owner[before][0]].split:
                    before -= SLOTS
                if before >= 0:
                    v = linear(lambda x: done[x][1], before, per, i, iterations)
                    act.wait_ge(out_ready if done[before][0] == "out" else part_used, v)
                f(w_hi[:, slot, 0:n], raw[:, slot, 0:n], ACT.Copy).then_inc(hi_split, 1)

            def split_ahead(k, o):
                last = min(first_chunk[k] + stages[k].chunk_of(o)[-1] + AHEAD, n_chunks - 1)
                while split_to[0] <= last:
                    if stages[owner[split_to[0]][0]].split:
                        split(split_to[0])
                    split_to[0] += 1

            def deviation(dst, src, n, eps):
                stat.expect()
                std.did(f(dst, src, ACT.Sqrt, bias=eps, scale=1.0 / n))

            def read_out(k, o, i=None, iterations=1):
                s = stages[k]
                name = s.name
                g = first_out[k] + o
                if name == "ffn_in" and o % 2 == 0:
                    n = o // 2
                    act.wait_ge(read_dve, linear(lambda x: freed[x][1], g, 4, i, iterations))
                    silus.did(f(silu[:, n % 2, 0:T], scaled[:, n % 2, :], ACT.Silu))
                elif name == "lru_gate":
                    act.wait_ge(read_dve, freed[g][1])
                    to_dve.did(f(lr_g[:, o, :], lr_g[:, o, :], ACT.Gelu_apprx_tanh))
                elif name == "ml_in" and 1 <= o < 9:
                    from_dve.expect()
                    if o < 5:
                        to_dve.did(f(ml_q[:, o - 1, :], ml_cv[:, o % 2, 0, :], ACT.Silu))
                    else:
                        to_dve.did(f(ml_k[:, o - 5, :], ml_cv[:, o % 2, :, :].rearrange("p a t -> p (a t)"), ACT.Silu))
                elif s.readers[o] == "act":
                    act.wait_ge(out_ready, linear(lambda x: x + 1, g, 4, i, iterations))
                    bank = ps[:, g % BANKS, 0:(s.cols[o] if s.cols else s.width)]
                    if name == "lru_gates":
                        n = o // 2
                        if o % 2 == 0:
                            ins = f(lr_r[:, n, :], bank, ACT.Sigmoid, bias=param("gate_a_b", n))
                        else:
                            ins = f(lr_i[:, n, :], bank, ACT.Sigmoid, bias=param("gate_x_b", n))
                    elif name == "ffn_in_2":
                        n = o // 2
                        if n >= 2 or i is not None:
                            act.wait_ge(read_dve, linear(lambda x: freed[x][1], g - 3, 4, i, iterations))
                        ins = f(silu[:, n % 2, 0:s.width], bank, ACT.Silu)
                    else:
                        ins = f(ml_og[:, o - 17, :], bank, ACT.Sigmoid)
                    ins.then_inc(read_act, 1)

            def layer_norm(w):
                stat.skip()
                base = sq_used.n
                for o in range(KD):
                    from_dve.expect()
                    if o >= 2:
                        sq_used.need(base + o - 1)
                    sq.did(f(silu[:, o % 2, 0:w], res[:, o, 0:w], ACT.Square))
                sq_used.skip(KD)
                sq_used.need(sq_used.n)
                std.did(f(rstd[:, 0:w], ps[:, 5, 0:w], ACT.Sqrt, bias=const("eps_ln"), scale=1.0 / D))

            def log_sigmoid(t):
                from_dve.expect()
                to_dve.did(f(t[1], t[0], ACT.Exp))
                from_dve.expect()
                to_dve.did(f(t[0], t[2], ACT.Ln))

            def transposes(dst, jobs):
                for n in range(jobs // 4):
                    from_pe.expect()
                    to_pe.did(f(dst[:, n * 512:n * 512 + 512], ps[:, 6 + n % 2, :], ACT.Copy))

            def head_norms(n, width):
                stat.expect()
                std.did(f(hn_rs[:, 0:width], ps[0:32, 4, 0:width], ACT.Sqrt, bias=const("eps", rows=32),
                          scale=const("row_scale", rows=32)))
                from_pe.skip(n)

            def attention(units, groups, scale, masked):
                u0, g0 = cnt["u"], cnt["g"]

                def weights(u):
                    keys = units[u][1]
                    m = so_m[:, u % 2, :]
                    act.wait_ge(max_ready, u0 + u + 1)
                    if u >= 2:
                        act.wait_ge(transposed, u0 + u - 1)
                    src = so_s[:, u % 2, 0:keys] if masked else ps[:, 4 + u % 2, 0:keys]
                    f(so_p[:, u % 2, 0:keys], src, ACT.Exp, bias=m[:, 0:1], scale=1.0 if masked else scale,
                      accum_out=m[:, 2:3]).then_inc(probs_ready, 1)

                def turn(u):
                    keys, g = units[u][1], u // 2
                    act.wait_ge(transposed, u0 + u + 1)
                    if g >= 2:
                        act.wait_ge(pv_done, g0 + g - 1)
                    a = (u % 2) * P
                    f(so_pt[:, g % 2, 0:keys // P, a:a + P],
                      ps[:, 6 + u % 2, 0:keys].rearrange("p (k q) -> p k q", q=P), ACT.Copy).then_inc(turned, 1)

                weights(0)
                for u in range(len(units)):
                    if u + 1 < len(units):
                        weights(u + 1)
                    turn(u)
                cnt["u"] += len(units)
                cnt["g"] += len(groups)

            def mlstm():
                r = [ml_row[:, n, :] for n in range(5)]
                log_sigmoid([r[2], r[3], r[4]])
                from_dve.expect()
                to_dve.did(f(r[4][:, 0:T], r[4][:, 0:T], ACT.Exp, scale=-1.0))
                from_pe.skip(1)
                for h in range(4):
                    from_pe.skip(1)
                    for d in range(2):
                        from_pe.skip(2)
                        from_dve.expect()
                        n_at = 0
                        for n, (t, a, w, m) in enumerate(lat_keys(d)):
                            if m is None:
                                src = ps[:, 4, 0:T]
                            else:
                                src, n_at = ml_msk[:, n_at:n_at + w], n_at + w
                            col = 32 * d + h
                            ins = f(ml_e[:, n, 0:w], src, ACT.Exp, bias=ml_col[:, t, col:col + 1], scale=-1.0)
                        to_dve.did(ins)
                from_pe.skip(4)
                for h in range(4):
                    from_dve.expect()
                    for v in range(2):
                        ins = f(ml_sq(h, v), ml_h[:, 2 * h + v, :], ACT.Square)
                    to_pe.did(ins)
                for h in range(4):
                    from_pe.expect()
                    to_dve.did(f(ml_q[:, h, :], ps[:, 4 + h, 0:T], ACT.Sqrt, bias=const("eps_ln"), scale=0.5 / P))

            def run(k):
                s = stages[k]
                count = sum(bodies(k, AHEAD)[:2]) if s.name in ("ffn_in", "ffn_in_2") else 0
                o = 0
                if count:
                    for o in range(4):
                        split_ahead(k, o)
                        read_out(k, o)
                    with act.Fori(0, count - 1) as i:
                        silus.enter(i, 2 if s.name == "ffn_in" else 0)
                        for o in range(4, 8):
                            split(first_chunk[k] + o + AHEAD, i, count - 1, 4)
                            read_out(k, o, i, count - 1)
                        silus.leave(count - 1)
                    split_to[0] += 4 * (count - 1)
                    o = 4 * count
                for o in range(o, s.outs):
                    split_ahead(k, o)
                    read_out(k, o)

            act.wait_ge(inputs_landed, 48)
            log_sigmoid([decay_c[:, n, :] for n in range(3)])
            from_dve.expect()
            a = PARAM_AT["cond"]
            to_pe.did(f(cond[:], par[:, a:a + 2 * KD].rearrange("p (k v) -> p k v", v=2), ACT.Silu))
            for k, s in enumerate(stages):
                name = s.name
                if name == "ada":
                    continue
                if name in ("conv_c", "lru_rec", "mla_down", "ffn_in"):
                    split_ahead(k, 0)
                    deviation(rstd[:, 0:T], ps[:, 4, 0:T], D, const("eps"))
                elif name == "mla_uq":
                    deviation(ma_rs[:, 0, :], ps[:, 4, 0:T], Q_RANK, const("eps"))
                    deviation(ma_rs[:, 1, :], ps[:, 5, 0:T], KV_RANK, const("eps"))
                    from_dve.expect()
                    f(ma_sin[:], ma_ang[:, 0, :], ACT.Sin)
                    to_dve.did(f(ma_cos[:], ma_ang[:, 2, :], ACT.Sin))
                run(k)
                if name == "lru_gates":
                    act.wait_ge(read_act, freed[first_out[k] + s.outs - 1][1])
                    for n in range(KL):
                        f(lr_a[:, n, :], lr_r[:, n, :], ACT.Exp, scale=decay_c[:, 4, n:n + 1])
                        to_dve.did(f(lr_t[:, n, :], lr_r[:, n, :], ACT.Tanh, scale=decay_c[:, 5, n:n + 1]))
                    for n in range(KL):
                        from_dve.expect()
                        to_dve.did(f(lr_t[:, n, :], lr_t[:, n, :], ACT.Sqrt))
                elif name == "mla_ukv":
                    transposes(ma_vt[:].rearrange("p a b -> p (a b)"), 2 * HEADS)
                    head_norms(len(mla_norms()), T)
                    from_pe.skip(len(mla_ropes))
                    attention(mla_units(), mla_groups(), (NOPE + ROPE) ** -0.5, True)
                elif name == "att_in":
                    transposes(ga_vt[:].rearrange("p a b -> p (a b)"), 8)
                    head_norms(len(gqa_norms()), T2)
                    from_pe.skip(len(gqa_ropes))
                    attention(gqa_units(), gqa_groups(), P ** -0.5, False)
                elif name == "ml_in":
                    transposes(ml_vt[:].rearrange("p a b -> p (a b)"), 4 * KD)
                    mlstm()
                elif name in ("ffn_out_2", "att_out", "ml_out"):
                    layer_norm(s.width)


def tiles(w):
    k, n = w.shape
    return w.reshape(k // P, P, n // P, P).transpose(2, 1, 0, 3).reshape(n // P, P, k)


def grouped(w, per):
    t = tiles(w)
    n, p, k = t.shape
    return t.reshape(n // per, per, p, k).transpose(0, 2, 1, 3).reshape(n // per, p, per * k)


def by_feature(v):
    v = v.reshape(-1, v.shape[-1] // P, P)
    return v.transpose(2, 0, 1).reshape(P, -1)


def gate_up(w, ff):
    k = w.shape[0]
    return w.reshape(k, 2, ff // P, P).transpose(0, 2, 1, 3).reshape(k, 2 * ff)


def constants():
    c = np.zeros((P, N_CONST), np.float32)
    p = np.arange(P)

    def put(name, v):
        c[:, CONST_AT[name]:CONST_AT[name] + CONST_SIZES[name]] = v

    put("ident", np.eye(P))
    put("ones", 1.0)
    rot = np.zeros((P, P), np.float32)
    for m in range(P):
        if m % 64 < 32:
            rot[m + 32, m] = -1.0
        else:
            rot[m - 32, m] = 1.0
    put("rot", rot)
    z = np.zeros((P, 63), np.float32)
    z[:, 31] = 1.0
    put("sel", z)
    z = np.zeros((P, 64), np.float32)
    z[:64, 31] = 1.0
    z[64:, 32] = 1.0
    put("sel2", z)
    put("eps", NORM_EPS)
    put("eps_ln", LN_EPS)
    inv = (10000.0 ** (-np.arange(0, ROPE, 2, dtype=np.float32) / ROPE)).astype(np.float32)
    put("inv_freq", inv[p % 32][:, None])
    scale = np.where(p < 16, 1.0 / NOPE, 1.0 / ROPE).astype(np.float32)
    put("row_scale", scale[:, None])
    mla = np.zeros((P, N_MLA_CONST), np.float32)
    for n in range(5):
        mla[16 + 2 * n, n * P:n * P + 64] = 1.0
        mla[17 + 2 * n, n * P + 64:n * P + P] = 1.0
    q, key = p[:, None], p[None, :]
    mla[:, 6 * P:] = np.where(key <= q, 0.0, -BIG)
    ml = np.zeros((P, N_ML_CONST), np.float32)
    s, t = p[:, None], p[None, :]
    ml[:, 0:P] = np.where(s <= t, 0.0, BIG)
    ml[:, 2 * P:] = np.where(s >= t, 0.0, BIG)
    pos = np.arange(T)
    rope = np.zeros((P, 2, T), np.float32)
    inv = (10000.0 ** (-np.arange(32, dtype=np.float32) / 32)).astype(np.float32)
    for m in range(P):
        where = (pos // 64 if m < 64 else pos % 64).astype(np.float32)
        ang = where * inv[m % 32]
        rope[m, 0], rope[m, 1] = np.cos(ang), np.sin(ang)
    return c, mla, ml, rope


def _lay_out(a):
    f = {}
    cat = np.concatenate
    f["x"] = a["x"][0].T.reshape(KD, P, T).transpose(1, 0, 2)
    f["ctx"] = a["ctx_2"][0].T.reshape(KD, P, T).transpose(1, 0, 2)
    f["positions"] = a["positions"].reshape(1, T)
    f["w_conv_in"] = cat([tiles(w[:, n * D:(n + 1) * D]) for w in a["conv_w_in"] for n in (1, 2, 0)])
    f["w_conv_out"] = cat([tiles(w) for w in a["conv_w_out"]])
    w = a["lru_w_in"][0]
    f["w_lru_in"] = cat([tiles(w[:, LRU:]), tiles(w[:, :LRU])])
    gates = np.stack([a["lru_gate_a_w"][0], a["lru_gate_x_w"][0]], 1).reshape(2 * KL, P, P)
    f["w_lru_gates"] = gates.reshape(5, 4, P, P).transpose(0, 2, 1, 3).reshape(5, P, 4 * P)
    f["w_lru_out"] = tiles(a["lru_w_out"][0])
    w = a["mla_w_down"][0]
    f["w_mla_down"] = tiles(cat([w, w[:, Q_RANK + KV_RANK:]], axis=1))
    w = a["mla_w_uq"][0].reshape(Q_RANK, HEADS, NOPE + ROPE)
    w = cat([w[:, :, :NOPE].reshape(Q_RANK, -1), w[:, :, NOPE:].reshape(Q_RANK, -1)], axis=1)
    f["w_mla_uq"] = grouped(w, 2)
    w = a["mla_w_ukv"][0].reshape(KV_RANK, HEADS, 2, P)
    f["w_mla_ukv"] = grouped(w.transpose(0, 2, 1, 3).reshape(KV_RANK, -1), 4)
    f["w_mla_o"] = tiles(a["mla_w_o"][0])
    f["w_ffn_in"] = cat([tiles(gate_up(w, FF)) for w in a["ffn_w_gu"]])
    f["w_ffn_out"] = cat([tiles(w) for w in a["ffn_w_down"]])
    f["w_ada"] = cat([tiles(w) for w in a["ada_w_2"]])
    f["w_ffn_in_2"] = cat([tiles(gate_up(w, FF)) for l in a["ffn_w_in_2"] for w in l])
    f["w_ffn_out_2"] = cat([tiles(w) for l in a["ffn_w_out_2"] for w in l])
    f["w_att_in"] = tiles(a["att_w_in_2"][0])
    f["w_att_out"] = tiles(a["att_w_out_2"][0])
    w = a["ml_w_in_2"][0]
    g = w[:, 3072:].reshape(D, 4, 4)
    gt = np.zeros((D, P), np.float32)
    for kind, at in ((0, 0), (2, 32), (1, 64), (3, 96)):
        gt[:, at:at + 4] = g[:, kind]
    f["w_ml_in"] = tiles(cat([gt, w[:, :3072]], axis=1))
    f["w_ml_out"] = tiles(a["ml_w_out_2"][0])

    par = np.zeros((P, N_PARAM), np.float32)

    def put(name, v):
        par[:, PARAM_AT[name]:PARAM_AT[name] + PARAM_SIZES[name]] = v

    put("mix_norm", by_feature(a["mix_norm"]))
    put("ffn_norm", by_feature(a["ffn_norm"]))
    put("conv_w", a["conv_w"].reshape(2, 3, KD, P).transpose(3, 0, 2, 1).reshape(P, -1))
    put("lru_conv_w", a["lru_conv_w"].reshape(4, KL, P).transpose(2, 1, 0).reshape(P, -1))
    put("lru_conv_b", by_feature(a["lru_conv_b"]))
    put("gate_a_b", a["lru_gate_a_b"][0].T)
    put("gate_x_b", a["lru_gate_x_b"][0].T)
    put("lam", by_feature(a["lru_lambda"]))
    put("q_norm", by_feature(a["mla_q_norm"]))
    put("kv_norm", by_feature(a["mla_kv_norm"]))
    put("qn_norm", a["mla_qn_norm"].T)
    put("kn_norm", a["mla_kn_norm"].T)
    put("qr_norm", cat([a["mla_qr_norm"]] * 2, axis=1).T)
    put("kr_norm", cat([a["mla_kr_norm"]] * 2, axis=1).T)
    put("ada_b", by_feature(a["ada_b_2"]))
    put("ln_g", by_feature(a["ln_g_2"]))
    put("ln_b", by_feature(a["ln_b_2"]))
    put("att_q_gain", a["att_q_gain_2"].T)
    put("att_k_gain", a["att_k_gain_2"].T)
    put("ml_conv_w", a["ml_conv_w_2"].reshape(3, 8, P).transpose(2, 1, 0).reshape(P, -1))
    put("ml_conv_b", by_feature(a["ml_conv_b_2"]))
    put("ml_norm_g", by_feature(a["ml_norm_g_2"]))
    b = a["ml_gate_b_2"].reshape(4, 4)
    for name, (fwd, bwd) in (("ml_bias_i", (0, 2)), ("ml_bias_f", (1, 3))):
        par[0:4, PARAM_AT[name]] = b[fwd]
        par[32:36, PARAM_AT[name]] = b[bwd]
    both = np.stack([a["c_2"].reshape(KD, P), a["c_ctx_2"].reshape(KD, P)], 0)
    put("cond", both.transpose(2, 1, 0).reshape(P, -1))
    f["params"] = par
    f["consts"], f["mla_consts"], f["ml_consts"], f["gqa_rope"] = constants()
    return {n: np.ascontiguousarray(v) for n, v in f.items()}


def kernel(**inputs):
    import concourse.bacc as bacc
    from concourse.bass_utils import run_bass_kernel_spmd

    laid = _lay_out({n: np.asarray(v) for n, v in inputs.items()})
    nc = bacc.Bacc("TRN2", target_bir_lowering=False, num_devices=1)
    dram = {n: nc.dram_tensor(f"in_{n}", v.shape, mybir.dt.from_np(v.dtype), kind="ExternalInput").ap()
            for n, v in laid.items()}
    out = nc.dram_tensor("out_y", (P, KD, T), F32, kind="ExternalOutput").ap()
    build_blocks(nc, dram, out)
    r = run_bass_kernel_spmd(nc, [{f"in_{n}": v for n, v in laid.items()}], core_ids=[0])
    y = np.asarray(r.results[0]["out_y"])
    return y.transpose(1, 0, 2).reshape(D, T).T.reshape(1, T, D)
```

```python
from contextlib import ExitStack
import math

import numpy as np

import concourse.bass as bass
from concourse import mybir

P = 128
D = 1024
T = 256
T2 = 2 * T
KD = D // P
FF = 2816
KF = FF // P
LRU = 1280
KL = LRU // P
DEPTH, DEPTH_2 = 4, 2
HEADS, ROPE, NOPE = 8, 64, 128
Q_RANK, KV_RANK = 384, 256
N_MOD = 9
ALPHA = (2.0 * DEPTH_2) ** 0.25
NORM_EPS, LN_EPS = 1e-6, 1e-5
BIG = 1e30

SLOTS = 4
CHUNK = 8
AHEAD = 3
RING = 3
SCORE_BANKS = (4, 5, 2)
FIRST_SPLITS = (2, 4, 6)
BANKS = 4

MOD_WIDTH = 512
MOD_GROUPS = DEPTH_2 * N_MOD * D // MOD_WIDTH
MOD_BODIES = MOD_GROUPS // DEPTH
MOD_SLOTS = 4
MOD_AFTER = {0: (0, 1), 1: (2,), 2: (3,), 3: ()}

ALU = mybir.AluOpType
ACT = mybir.ActivationFunctionType
AX = mybir.AxisListType
F32 = mybir.dt.float32
F32R = mybir.dt.float32r
I32 = mybir.dt.int32

PARAM_SIZES = dict(
    mix_norm=DEPTH * KD, ffn_norm=DEPTH * KD, conv_w=2 * KD * 3,
    lru_conv_w=KL * 4, lru_conv_b=KL, gate_a_b=KL, gate_x_b=KL, lam=KL,
    q_norm=3, kv_norm=2, qn_norm=1, qr_norm=1, kn_norm=1, kr_norm=1,
    ada_b=2 * 72, ln_g=2 * 3 * KD, ln_b=2 * 3 * KD, att_q_gain=1, att_k_gain=1,
    ml_conv_w=8 * 3, ml_conv_b=8, ml_norm_g=KD, ml_bias_i=1, ml_bias_f=1, cond=KD * 2,
)
PARAM_AT = {}
_n = 0
for _name, _size in PARAM_SIZES.items():
    PARAM_AT[_name] = _n
    _n += _size
N_PARAM = _n

CONST_SIZES = dict(ident=P, ones=P, rot=P, sel=63, sel2=64, eps=1, eps_ln=1, fold=2, inv_freq=1, row_scale=1)
CONST_AT = {}
_n = 0
for _name, _size in CONST_SIZES.items():
    CONST_AT[_name] = _n
    _n += _size
N_CONST = _n
N_MLA_CONST = 5 * P + 2 * P
N_ML_CONST = 3 * P


class Product:

    def __init__(self, name, outs, ktiles, width, weights, row=0, cuts=None, per_chunk=1, cols=None,
                 readers=None, mods=None):
        self.name, self.outs, self.ktiles, self.width = name, outs, ktiles, width
        self.weights, self.row = weights, row
        self.cuts = cuts or [(0, ktiles)]
        self.per_chunk = per_chunk
        self.cols = cols
        self.readers = readers or ["dve"] * outs
        self.mods = mods
        if per_chunk > 1:
            self.n_chunks = -(-outs // per_chunk)
        else:
            self.n_chunks = outs * len(self.cuts)

    def chunk_of(self, o):
        if self.per_chunk > 1:
            return [o // self.per_chunk]
        n = len(self.cuts)
        return list(range(o * n, o * n + n))

    def tiles_of(self, j):
        if self.per_chunk > 1:
            return [(o, k) for o in range(j * self.per_chunk, min((j + 1) * self.per_chunk, self.outs))
                    for k in range(self.ktiles)]
        n = len(self.cuts)
        return [(j // n, k) for k in range(*self.cuts[j % n])]


FF_CUTS = [(0, 6), (6, 12), (12, 17), (17, 22)]
LRU_CUTS = [(0, 5), (5, 10)]
GU_READERS = ["act", "dve"] * KF
NORMED = ("conv_c", "lru_rec", "mla_down", "ffn_in")
FRESH = dict(conv_c=KD, conv_h=0, conv_b=0, conv_out=KD, lru_rec=KD, lru_gate=0, lru_gates=KL, lru_out=KL,
             mla_down=KD, mla_uq=3, mla_ukv=2, mla_out=KD, ffn_in=KD, ffn_out=KF, ffn_in_2=KD, ffn_out_2=KF,
             att_in=KD, att_out=2 * HEADS, ml_in=KD, ml_out=KD)


def plan():
    s = []
    for i in range(DEPTH):
        kind, j = i % 3, i // 3
        if kind == 0:
            for part, name in enumerate(("conv_c", "conv_h", "conv_b")):
                s.append(Product(name, KD, KD, T, "w_conv_in", row=(3 * j + part) * KD))
            s.append(Product("conv_out", KD, KD, T, "w_conv_out", row=j * KD))
        elif kind == 1:
            s.append(Product("lru_rec", KL, KD, T, "w_lru_in", row=0))
            s.append(Product("lru_gates", 2 * KL, 1, T, "w_lru_gates", per_chunk=4, readers=["act"] * 2 * KL))
            s.append(Product("lru_gate", KL, KD, T, "w_lru_in", row=KL))
            s.append(Product("lru_out", KD, KL, T, "w_lru_out", cuts=LRU_CUTS))
        else:
            s.append(Product("mla_down", 6, KD, T, "w_mla_down"))
            s.append(Product("mla_uq", 12, 3, T, "w_mla_uq", per_chunk=2))
            s.append(Product("mla_ukv", 16, 2, T, "w_mla_ukv", per_chunk=4))
            s.append(Product("mla_out", KD, KD, T, "w_mla_o"))
        s.append(Product("ffn_in", 2 * KF, KD, T, "w_ffn_in", row=i * 2 * KF, mods=i * MOD_BODIES))
        s.append(Product("ffn_out", KD, KF, T, "w_ffn_out", row=i * KD, cuts=FF_CUTS))
    for i in range(DEPTH_2):
        w = T2
        s.append(Product("ffn_in_2", 2 * KF, KD, w, "w_ffn_in_2", row=2 * i * 2 * KF, readers=GU_READERS))
        s.append(Product("ffn_out_2", KD, KF, w, "w_ffn_out_2", row=2 * i * KD, cuts=FF_CUTS))
        if i == 0:
            s.append(Product("att_in", 12, KD, T2, "w_att_in"))
            s.append(Product("att_out", KD, KD, T2, "w_att_out"))
        else:
            s.append(Product("ml_in", 25, KD, T2, "w_ml_in",
                             cols=[T2] + [T] * 4 + [T2] * 4 + [T2] * 8 + [T] * 8,
                             readers=["dve"] * 17 + ["act"] * 8))
            s.append(Product("ml_out", KD, KD, T, "w_ml_out"))
            w = T
        s.append(Product("ffn_in_2", 2 * KF, KD, w, "w_ffn_in_2", row=(2 * i + 1) * 2 * KF, readers=GU_READERS))
        s.append(Product("ffn_out_2", KD, KF, w, "w_ffn_out_2", row=(2 * i + 1) * KD, cuts=FF_CUTS))
    return s


class Tally:

    def __init__(self, engine, sem):
        self.engine, self.sem, self.n, self.i, self.per = engine, sem, 0, None, 0

    def at(self, n):
        return n if self.i is None else n + self.i * self.per

    def did(self, ins, by=1):
        ins.then_inc(self.sem, by)
        self.n += by
        return self.n

    def expect(self, by=1):
        self.n += by
        self.engine.wait_ge(self.sem, self.at(self.n))
        return self.n

    def need(self, n):
        if n > 0:
            self.engine.wait_ge(self.sem, self.at(n))

    def skip(self, n=1):
        self.n += n

    def link(self, ins):
        self.need(self.did(ins))

    def enter(self, i, per):
        self.i, self.per, self.start = i, per, self.n

    def leave(self, iterations):
        assert self.n - self.start == self.per, (self.n - self.start, self.per)
        self.n, self.i = self.start + self.per * iterations, None


def build_blocks(nc, dram, out):
    stages = plan()
    first_out, first_chunk, o, c = [], [], 0, 0
    for s in stages:
        first_out.append(o)
        first_chunk.append(c)
        o, c = o + s.outs, c + s.n_chunks
    n_chunks = c
    operands_before = [sum(FRESH[x.name] for x in stages[:k]) for k in range(len(stages) + 1)]
    owner = [(k, j) for k, s in enumerate(stages) for j in range(s.n_chunks)]
    freed, tally = [], {"dve": 0, "act": 0}
    for s in stages:
        for e in s.readers:
            tally[e] += 1
            freed.append((e, tally[e]))

    done, parts = [], 0
    for c, (k, j) in enumerate(owner):
        s = stages[k]
        to, kk = s.tiles_of(j)[-1]
        if kk == s.ktiles - 1:
            done.append(("out", first_out[k] + to + 1))
        else:
            parts += 1
            done.append(("part", parts))

    def linear(value, at, step, i, iterations):
        v = value(at)
        if i is None:
            return v
        d = value(at + step) - v
        assert all(value(at + step * m) == v + d * m for m in range(iterations))
        return v + i * d if d else v

    def bodies(k, ahead=0):
        s = stages[k]
        per = 4 // s.per_chunk if s.per_chunk > 1 else 4 * len(s.cuts)
        plain = k > 0 and s.name not in NORMED and all(set(x.readers) == {"dve"} for x in stages[k - 1:k + 1])
        start = 0 if plain else 1
        n = 0
        if s.cols:
            return 0, 0, per
        while (start + n + 1) * 4 <= s.outs and (start + n + 1) * per + ahead <= s.n_chunks:
            n += 1
        return (start, n, per) if n >= 2 and per % SLOTS == 0 else (start, 0, per)

    ctx = ExitStack()
    with ctx:
        def sem(name):
            return ctx.enter_context(nc.semaphore(name))

        place = [nc.sbuf_base + (-nc.sbuf_base) % 32]

        def sb(name, shape, dt=F32, at=None):
            where = place if at is None else at
            t = nc.alloc_sbuf_tensor_at(name, shape, dt, offset=where[0])
            size = 4
            for x in shape[1:]:
                size *= x
            where[0] += size + (-size) % 32
            assert where[0] <= nc.sbuf_usable_end, (name, where[0], nc.sbuf_usable_end)
            return t

        raw = sb("raw", [P, SLOTS, CHUNK * P])
        w_hi = sb("w_hi", [P, SLOTS, CHUNK * P], F32R)
        w_lo = sb("w_lo", [P, SLOTS, CHUNK * P], F32R)
        res = sb("res", [P, KD, T2])
        x_hi_at = place[0]
        x_hi = sb("x_hi", [P, KD, T2], F32R)
        x_lo_at = place[0]
        x_lo = sb("x_lo", [P, KD, T2], F32R)
        scaled = sb("scaled", [P, 2, T])
        silu = sb("silu", [P, 2, T2])
        mod_rows = silu[0:4, :, T:T2]
        up = sb("up", [P, T])
        prod = sb("prod", [P, T2])
        acc = sb("acc", [P, T2])
        rstd = sb("rstd", [P, T2])
        par = sb("par", [P, N_PARAM])
        cst = sb("cst", [P, N_CONST])
        squares = nc.alloc_sbuf_tensor_at("squares", [P, KD, T2], F32, offset=x_lo_at)
        mod_w = nc.alloc_sbuf_tensor_at("mod_w", [P, 2 * KD, T2], F32, offset=x_hi_at)
        cond = sb("cond", [P, KD, 2])
        cond_parts = sb("cond_parts", [P, KD, 4], F32R)
        mod = sb("mod", [P, DEPTH_2, 72, 2])
        decay_c = sb("decay_c", [P, 6, KL])
        region = place[0]

        at = [region]
        h_hi = sb("h_hi", [P, KF, T2], F32R, at)
        h_lo = sb("h_lo", [P, KF, T2], F32R, at)
        mod_w_hi, mod_w_lo = h_hi[:, 0:4 * MOD_SLOTS, T:T2], h_lo[:, 0:4 * MOD_SLOTS, T:T2]

        at = [region]
        cv_c = sb("cv_c", [P, KD, T], F32, at)
        cv_x = sb("cv_x", [P, KD, T + 2], F32, at)
        cv_y = sb("cv_y", [P, KD, T], F32, at)
        cv_hi = sb("cv_hi", [P, KD, T], F32R, at)
        cv_lo = sb("cv_lo", [P, KD, T], F32R, at)

        at = [region]
        lr_pad = sb("lr_pad", [P, 2, T + 3], F32, at)
        lr_rec = sb("lr_rec", [P, KL, T], F32, at)
        lr_rec_hi = sb("lr_rec_hi", [P, KL, T], F32R, at)
        lr_rec_lo = sb("lr_rec_lo", [P, KL, T], F32R, at)
        lr_r = sb("lr_r", [P, KL, T], F32, at)
        lr_i = sb("lr_i", [P, KL, T], F32, at)
        lr_a = sb("lr_a", [P, KL, T], F32, at)
        lr_t = sb("lr_t", [P, KL, T], F32, at)
        lr_g = sb("lr_g", [P, KL, T], F32, at)
        lr_o_hi, lr_o_lo = lr_rec_hi, lr_rec_lo

        at = [region]
        ma_q = sb("ma_q", [P, 12, T], F32, at)
        ma_k = sb("ma_k", [P, 9, T], F32, at)
        ma_v = sb("ma_v", [P, HEADS, T], F32, at)
        ma_vt = sb("ma_vt", [P, 2, HEADS * P], F32, at)
        ma_o_hi = sb("ma_o_hi", [P, HEADS, T], F32R, at)
        ma_o_lo = sb("ma_o_lo", [P, HEADS, T], F32R, at)
        ma_const = sb("ma_const", [P, N_MLA_CONST], F32, at)
        ma_pos = sb("ma_pos", [P, T], I32, at)
        ma_cos = sb("ma_cos", [P, T], F32, at)
        ma_sin = sb("ma_sin", [P, T], F32, at)
        ma_ang = sb("ma_ang", [P, 3, T], F32, at)
        work = list(at)
        ma_x_hi = sb("ma_x_hi", [P, 5, T], F32R, at)
        ma_x_lo = sb("ma_x_lo", [P, 5, T], F32R, at)
        work_2 = list(at)
        ma_acc = sb("ma_acc", [P, 2, T], F32, at)
        ma_rs = sb("ma_rs", [P, 2, T], F32, at)
        after_mla = list(at)

        at = [region]
        ga_rope = sb("ga_rope", [P, 2, T], F32, at)
        ga_q = sb("ga_q", [P, HEADS, T2], F32, at)
        ga_k = sb("ga_k", [P, 2, T2], F32, at)
        ga_v = sb("ga_v", [P, 2, T2], F32, at)
        ga_vt = sb("ga_vt", [P, 4, 2 * P], F32, at)

        so_pt = sb("so_pt", [P, 2, 4, T], F32, work)
        so_s = sb("so_s", [P, RING, T], F32, list(work_2))
        hn_sq = sb("hn_sq", [P, 2, T2], F32, work_2)
        at = after_mla
        hn_rs = sb("hn_rs", [32, T2], F32, at)
        rp = sb("rp", [P, 2, T], F32, at)
        so_p = sb("so_p", [P, RING, T2], F32, at)
        so_m = sb("so_m", [P, RING, 4], F32, at)

        at = [region]
        ml_const = sb("ml_const", [P, N_ML_CONST], F32, at)
        ml_pad = sb("ml_pad", [P, 2, T + 2], F32, at)
        ml_cv = sb("ml_cv", [P, 2, 2, T], F32, at)
        ml_q = sb("ml_q", [P, 4, T], F32, at)
        ml_k = sb("ml_k", [P, 4, T2], F32, at)
        ml_vt = sb("ml_vt", [P, 4, D], F32, at)
        ml_og = sb("ml_og", [P, KD, T], F32, at)
        ml_row = sb("ml_row", [64, 5, T2], F32, at)
        ml_col = sb("ml_col", [P, 4, 64], F32, at)
        ml_den = sb("ml_den", [P, 2, T], F32, at)
        ml_msk = sb("ml_msk", [P, 2, 3 * P], F32, at)
        shared = at[0]
        ml_v = sb("ml_v", [P, KD, T2], F32, at)
        at = [shared]
        ml_h = sb("ml_h", [P, KD, T], F32, at)
        ml_e = sb("ml_e", [P, 2, 4, T], F32, at)
        ml_pt = sb("ml_pt", [P, 2, 4, T], F32, at)

        ps = ctx.enter_context(nc.psum_tensor("ps", [P, 8, 512], F32))

        landed = [sem(f"weights_landed_{i}") for i in range(SLOTS)]
        hi_split = sem("hi_split")
        lo_split = sem("lo_split")
        part_used = sem("part_used")
        out_ready = sem("out_ready")
        read_dve = sem("read_dve")
        read_act = sem("read_act")
        operand_ready = sem("operand_ready")
        dve_step = sem("dve_step")
        act_step = sem("act_step")
        inputs_landed = sem("inputs_landed")
        region_free = sem("region_free")
        consts_landed = sem("consts_landed")
        mod_landed = [sem(f"mod_landed_{i}") for i in range(MOD_SLOTS)]
        mod_hi_split = sem("mod_hi_split")
        mod_lo_split = sem("mod_lo_split")
        mod_used = sem("mod_used")
        mod_rows_copied = sem("mod_rows_copied")
        mod_turned = sem("mod_turned")
        mod_read = sem("mod_read")
        silu_ready = sem("silu_ready")
        sums_ready = sem("sums_ready")
        stat_ready = sem("stat_ready")
        std_ready = sem("std_ready")
        act_ready = sem("act_ready")
        dve_ready = sem("dve_ready")
        pe_ready = sem("pe_ready")
        squares_ready = sem("squares_ready")
        squares_used = sem("squares_used")
        scores_ready = sem("scores_ready")
        max_ready = sem("max_ready")
        probs_ready = sem("probs_ready")
        probs_scaled = sem("probs_scaled")
        transposed = sem("transposed")
        turned = sem("turned")
        pv_done = sem("pv_done")
        head_squares = sem("head_squares")
        head_squares_used = sem("head_squares_used")
        ml_scores_ready = sem("ml_scores_ready")
        ml_rows_ready = sem("ml_rows_ready")
        ml_masked_ready = sem("ml_masked_ready")
        ml_decays_ready = sem("ml_decays_ready")
        ml_weights_ready = sem("ml_weights_ready")
        ml_values_ready = sem("ml_values_ready")
        ml_values_read = sem("ml_values_read")
        gelu_ready = sem("gelu_ready")
        for_act = sem("for_act")
        for_dve = sem("for_dve")
        result_ready = sem("result_ready")
        stored = sem("stored")

        def const(name, n=None, rows=P):
            a = CONST_AT[name]
            return cst[0:rows, a:a + (n or CONST_SIZES[name])]

        def param(name, i=0, rows=P):
            a = PARAM_AT[name] + i
            return par[0:rows, a:a + 1]

        ones = const("ones")

        OPERAND = dict(conv_out=(cv_hi, cv_lo, 0), lru_gates=(lr_rec_hi, lr_rec_lo, 0),
                       lru_out=(lr_o_hi, lr_o_lo, 0), mla_uq=(ma_x_hi, ma_x_lo, 0),
                       mla_ukv=(ma_x_hi, ma_x_lo, 3), mla_out=(ma_o_hi, ma_o_lo, 0),
                       ffn_out=(h_hi, h_lo, 0), ffn_out_2=(h_hi, h_lo, 0))

        def mla_norms():
            sel = [ma_const[0:32, P * n:P * n + P] for n in range(5)]
            one = [const("ident", rows=32)[:, r:r + 1].to_broadcast([32, P]) for r in range(16)]
            return ([(ma_q[:, h, :], h, False, param("qn_norm"), one[h]) for h in range(8)]
                    + [(ma_k[:, h, :], 8 + h, False, param("kn_norm"), one[8 + h]) for h in range(8)]
                    + [(ma_q[:, 8 + n, :], 16 + 2 * n, True, param("qr_norm"), sel[n]) for n in range(4)]
                    + [(ma_k[:, 8, :], 24, True, param("kr_norm"), sel[4])])

        def gqa_norms():
            one = [const("ident", rows=32)[:, r:r + 1].to_broadcast([32, P]) for r in range(16)]
            return ([(ga_q[:, h, :], h, False, param("att_q_gain"), one[h]) for h in range(8)]
                    + [(ga_k[:, h, :], 8 + h, False, param("att_k_gain"), one[8 + h]) for h in range(2)])

        mla_ropes = [(ma_q[:, 8 + n, :]) for n in range(4)] + [ma_k[:, 8, :]]
        gqa_ropes = [ga_q[:, h, 0:T] for h in range(8)] + [ga_k[:, h, 0:T] for h in range(2)]

        def mla_units():
            units = []
            for h in range(HEADS):
                half = slice(64 * (h % 2), 64 * (h % 2) + 64)
                for i in range(2):
                    rows, keys = slice(i * P, i * P + P), (i + 1) * P
                    mask = ma_const[:, 5 * P + (1 - i) * P:7 * P]
                    units.append(([(ma_q[:, h, rows], ma_k[:, h, 0:keys]),
                                   (ma_q[half, 8 + h // 2, rows], ma_k[half, 8, 0:keys])], keys, mask))
            return units

        def gqa_units():
            units = []
            for h in range(HEADS):
                for i in range(4):
                    keys = slice(0, T2) if i < 2 else slice(T, T2)
                    units.append(([(ga_q[:, h, i * P:i * P + P], ga_k[:, h // 4, keys])],
                                  T2 if i < 2 else T, None))
            return units

        def mla_groups():
            return [([(ma_vt[:, kt, h * P:h * P + P], kt, kt * P) for kt in range(2)],
                     ma_o_hi[:, h, :], ma_o_lo[:, h, :]) for h in range(HEADS)]

        def gqa_groups():
            groups = []
            for h in range(HEADS):
                v = slice((h // 4) * P, (h // 4) * P + P)
                groups.append(([(ga_vt[:, kt, v], kt, 0) for kt in range(4)],
                               x_hi[:, h, 0:T], x_lo[:, h, 0:T]))
                groups.append(([(ga_vt[:, 2 + kt, v], kt, 0) for kt in range(2)],
                               x_hi[:, h, T:T2], x_lo[:, h, T:T2]))
            return groups

        def lat_keys(direction):
            if direction == 0:
                return [(2, 0, T, None), (3, 0, T, None), (0, 0, T, 0), (1, P, P, 0)]
            return [(2, 0, T, None), (3, 0, T, None), (1, 0, T, P), (0, 0, P, 2 * P)]

        ml_steps = [(h, d) for h in range(4) for d in range(2)]
        ML_ROWS, ML_NUM, ML_DEN = (4, 7), (5, 2), (6, 3)
        ML_SUM, ML_SQ = (0, 1, 5, 2), (4, 7, 6, 5)

        def ml_sq(h, v):
            n = 2 * h + v
            return ml_e[:, n // 4, n % 4, :]

        block = ctx.enter_context(nc.Block())

        @block.sync
        def _(sp):
            def small(dst, src):
                sp.dma_start(dst, src).then_inc(inputs_landed, 16)

            def load(k, j, i, iterations, per):
                s = stages[k]
                c = first_chunk[k] + j
                if c >= SLOTS:
                    v = linear(lambda x: x + 1, c - SLOTS, per, i, iterations)
                    sp.wait_ge(hi_split, v)
                    sp.wait_ge(lo_split, v)
                tiles = s.tiles_of(j)
                if s.per_chunk > 1:
                    row, a = s.row + j, 0
                    step = per
                else:
                    row, a = s.row + tiles[0][0], tiles[0][1] * P
                    step = 4
                n = len(tiles) * P
                src = dram[s.weights][row if i is None else row + i * step, :, a:a + n]
                sp.dma_start(raw[:, c % SLOTS, 0:n], src).then_inc(landed[c % SLOTS], 16)

            small(res[:, :, 0:T], dram["x"])
            small(par[:], dram["params"])
            small(cst[:], dram["consts"])
            for k, s in enumerate(stages):
                start, count, per = bodies(k)
                j = 0
                if count:
                    for j in range(start * per):
                        load(k, j, None, 1, per)
                    with sp.Fori(0, count) as i:
                        for j in range(per):
                            load(k, start * per + j, i, count, per)
                    j = (start + count) * per
                for j in range(j, s.n_chunks):
                    load(k, j, None, 1, per)
            for a in range(0, KD, 2):
                sp.wait_ge(result_ready, a + 2)
                sp.dma_start(out[:, a:a + 2, :], res[:, a:a + 2, 0:T]).then_inc(stored, 16)
            sp.wait_ge(stored, 16 * (KD // 2))

        @block.gpsimd
        def _(pool):
            pool.wait_ge(operand_ready, KD)
            pool.dma_start(res[:, :, T:T2], dram["ctx"]).then_inc(consts_landed, 16)
            pool.wait_ge(region_free, 1)
            pool.dma_start(ma_const[:], dram["mla_consts"]).then_inc(consts_landed, 16)
            pool.dma_start(ma_pos[:], dram["positions"].to_broadcast([P, T])).then_inc(consts_landed, 16)
            pool.wait_ge(region_free, 2)
            pool.dma_start(ga_rope[:], dram["gqa_rope"]).then_inc(consts_landed, 16)
            pool.wait_ge(region_free, 3)
            pool.dma_start(ml_const[:], dram["ml_consts"]).then_inc(consts_landed, 16)

        @block.tensor
        def _(pe):
            opnd = Tally(pe, operand_ready)
            sums = Tally(pe, sums_ready)
            stat = Tally(pe, stat_ready)
            from_dve = Tally(pe, dve_ready)
            from_act = Tally(pe, act_ready)
            mine = Tally(pe, pe_ready)
            sq_in, sq_out = Tally(pe, squares_ready), Tally(pe, squares_used)
            head_sq, head_sq_used = Tally(pe, head_squares), Tally(pe, head_squares_used)
            cnt = dict(u=0, g=0)

            def ones_sum(bank, src, width, last=True, start=True, stop=True):
                m = pe.matmul(ps[:, bank, 0:width], ones, src, start=start, stop=stop)
                if last:
                    stat.did(m)

            def output(k, o, i, iterations, per):
                s = stages[k]
                g = first_out[k] + o
                bank = g % BANKS
                hi, lo, base = OPERAND.get(s.name, (x_hi, x_lo, 0))
                width = s.cols[o] if s.cols else s.width
                dst = ps[:, bank, 0:width]
                if s.name == "lru_gates":
                    pe.wait_ge(operand_ready, operands_before[k] + o // 2 + 1)
                if g >= BANKS:
                    who = freed[g - BANKS][0]
                    v = linear(lambda x: freed[x][1], g - BANKS, 4, i, iterations)
                    pe.wait_ge(read_dve if who == "dve" else read_act, v)
                for j in s.chunk_of(o):
                    c = first_chunk[k] + j
                    tiles = s.tiles_of(j)
                    v = linear(lambda x: x + 1, c, per, i, iterations)
                    pe.wait_ge(hi_split, v)
                    pe.wait_ge(lo_split, v)
                    slot = c % SLOTS
                    for n, (to, kk) in enumerate(tiles):
                        if to != o:
                            continue
                        if o == 0 and kk < FRESH[s.name] and s.name not in ("mla_uq", "mla_ukv", "att_out"):
                            pe.wait_ge(operand_ready, operands_before[k] + kk + 1)
                        cols = slice(n * P, n * P + P)
                        x = kk + base if s.name != "lru_gates" else o // 2
                        xh, xl = hi[:, x, 0:width], lo[:, x, 0:width]
                        first, last = kk == 0, kk == s.ktiles - 1
                        pe.matmul(dst, w_hi[:, slot, cols], xh, start=first, stop=False)
                        pe.matmul(dst, w_hi[:, slot, cols], xl, start=False, stop=False)
                        m = pe.matmul(dst, w_lo[:, slot, cols], xh, start=False, stop=last)
                        if last:
                            m.then_inc(out_ready, 1)
                        elif n == len(tiles) - 1:
                            m.then_inc(part_used, 1)
                if s.mods is not None and 1 <= o // 4 <= MOD_BODIES:
                    modulation(s.mods + o // 4 - 1, o % 4, i)

            def modulation(g, o, i):
                for j in MOD_AFTER[o]:
                    n = MOD_SLOTS * g + j + 1
                    pe.wait_ge(mod_lo_split, n if i is None else n + i * MOD_SLOTS)
                    for kk in (2 * j, 2 * j + 1):
                        a = 4 * j + kk % 2 * 2
                        for w in (mod_w_hi, mod_w_lo):
                            m = pe.matmul(ps[0:4, 6, :].rearrange("p (a b) -> p a b", b=T), cond_parts[:, kk, :],
                                          w[:, a:a + 2, :], start=(kk == 0 and w is mod_w_hi),
                                          stop=(kk == KD - 1 and w is mod_w_lo))
                    m.then_inc(mod_used, 1)
                if o == 3:
                    pe.wait_ge(mod_rows_copied, g + 1 if i is None else g + 1 + i)
                    for n in range(4):
                        col = (4 * (g % (MOD_GROUPS // DEPTH_2)) + n) * 2
                        dst = ps[:, 7, slice(col, col + 2) if i is None else bass.ds(col + i * 8, 2)]
                        m = pe.matmul(dst, mod_rows[:, n // 2, n % 2 * P:n % 2 * P + P],
                                      const("fold", rows=4), start=True, stop=True)
                    m.then_inc(mod_turned, 1)

            def run(k):
                s = stages[k]
                start, count, per = bodies(k)

                def after(o):
                    if o == 0 and s.name in NORMED:
                        sums.expect()
                        ones_sum(4, acc[:, 0:T], T)

                o = 0
                if count:
                    for o in range(start * 4):
                        output(k, o, None, 1, per)
                        after(o)
                    if s.mods is not None:
                        count = MOD_BODIES
                    with pe.Fori(0, count) as i:
                        for o in range(4):
                            output(k, start * 4 + o, i, count, per)
                    o = (start + count) * 4
                for o in range(o, s.outs):
                    output(k, o, None, 1, per)
                    after(o)

            def layer_norm_sums(width):
                sums.expect()
                ones_sum(4, acc[:, 0:width], width)
                for o in range(KD):
                    sq_in.expect()
                    m = pe.matmul(ps[:, 5, 0:width], ones, squares[:, o, 0:width],
                                  start=(o == 0), stop=(o == KD - 1))
                sq_out.did(m)

            def head_norms(tiles, width):
                for n, (x, row, halves, gain, one) in enumerate(tiles):
                    head_sq.expect()
                    z = CONST_AT["sel2" if halves else "sel"] + 31 - row
                    m = pe.matmul(ps[0:32, 4, 0:width], cst[:, z:z + 32], hn_sq[:, n % 2, 0:width],
                                  start=(n == 0), stop=(n == len(tiles) - 1))
                    (head_sq_used if n < len(tiles) - 1 else stat).did(m)
                from_dve.expect()
                for n, (x, row, halves, gain, one) in enumerate(tiles):
                    if n >= 2:
                        from_dve.expect()
                    mine.did(pe.matmul(ps[:, 5 + n % 2, 0:width], one, hn_rs[:, 0:width], start=True, stop=True))
                from_dve.expect(min(2, len(tiles)))

            def ropes(tiles):
                for n, x in enumerate(tiles):
                    if n >= 2:
                        from_dve.expect()
                    mine.did(pe.matmul(ps[:, 4 + n % 2, 0:T], const("rot"), x, start=True, stop=True))
                from_dve.expect(3)

            def transposes(source, n_tiles, tokens, heads):
                jobs = [(tt, h) for tt in range(tokens) for h in range(heads)]
                for n in range(0, len(jobs), 4):
                    if n >= 8:
                        from_act.expect()
                    for q, (tt, h) in enumerate(jobs[n:n + 4]):
                        m = pe.transpose(ps[:, 6 + (n // 4) % 2, q * P:q * P + P],
                                         source[:, h, tt * P:tt * P + P], const("ident"))
                    mine.did(m)
                from_act.expect(min(2, len(jobs) // 4))

            def attention(units, groups):
                u0, g0 = cnt["u"], cnt["g"]

                def scores(u):
                    parts, keys, _ = units[u]
                    if u >= RING:
                        pe.wait_ge(probs_ready, u0 + u - RING + 1)
                    for n, (q, kx) in enumerate(parts):
                        m = pe.matmul(ps[:, SCORE_BANKS[u % RING], 0:keys], q, kx, start=(n == 0), stop=(n == len(parts) - 1))
                    m.then_inc(scores_ready, 1)

                def turn(u):
                    keys = units[u][1]
                    pe.wait_ge(probs_scaled, u0 + u + 1)
                    if u >= 2:
                        pe.wait_ge(turned, u0 + u - 1)
                    for kt in range(keys // P):
                        m = pe.transpose(ps[:, 6 + u % 2, kt * P:kt * P + P], so_p[:, u % RING, kt * P:kt * P + P],
                                         const("ident"))
                    m.then_inc(transposed, 1)

                def values(g):
                    pe.wait_ge(turned, u0 + 2 * g + 2)
                    if g >= 2:
                        pe.wait_ge(operand_ready, opnd.n + g - 1)
                    parts = groups[g][0]
                    for n, (v, kt, a) in enumerate(parts):
                        m = pe.matmul(ps[:, g % 2, a:T], v, so_pt[:, g % 2, kt, a:T], start=(n == 0),
                                      stop=(n == len(parts) - 1), skip_group_check=True)
                    m.then_inc(pv_done, 1)

                for u in range(RING - 1):
                    scores(u)
                for u in range(len(units)):
                    if u + RING - 1 < len(units):
                        scores(u + RING - 1)
                    turn(u)
                    if u % 2 == 0 and u >= 2:
                        values(u // 2 - 1)
                values(len(groups) - 1)
                cnt["u"] += len(units)
                cnt["g"] += len(groups)

            def mlstm():
                from_dve.expect()
                for t in range(4):
                    m = pe.transpose(ps[:, 4, 64 * t:64 * t + 64], ml_row[:, 2, t * P:t * P + P],
                                     const("ident", rows=64)[:, 0:64])
                mine.did(m)

                def scores(h):
                    if h:
                        pe.wait_ge(ml_weights_ready, 2 * h)
                    for t in range(4):
                        m = pe.matmul(ps[:, t // 2, (t % 2) * T:(t % 2) * T + T], ml_k[:, h, t * P:t * P + P],
                                      ml_q[:, h, :], start=True, stop=True)
                    m.then_inc(ml_scores_ready, 1)

                def to_all(j, source, banks, at):
                    h, d = ml_steps[j]
                    row = const("ident", rows=64)[:, 32 * d + h:32 * d + h + 1].to_broadcast([64, P])
                    return pe.matmul(ps[:, banks[j % 2], at:at + T], row, ml_row[:, source, 0:T],
                                     start=True, stop=True)

                from_dve.expect()
                scores(0)
                from_dve.expect()
                for j in range(2):
                    to_all(j, 1, ML_ROWS, 0).then_inc(ml_rows_ready, 1)
                for j, (h, d) in enumerate(ml_steps):
                    if j >= 2:
                        pe.wait_ge(ml_values_read, j - 1)
                    to_all(j, 4, ML_DEN, T)
                    pe.wait_ge(ml_weights_ready, j + 1)
                    for vt in range(2):
                        for n, (t, a, w, _) in enumerate(lat_keys(d)):
                            pe.matmul(ps[:, ML_NUM[j % 2], vt * T + a:vt * T + a + w],
                                      ml_vt[:, t, (2 * h + vt) * P:(2 * h + vt) * P + P],
                                      ml_pt[:, j % 2, n, 0:w], start=(n == 0), stop=(n == 3), skip_group_check=True)
                    for n, (t, a, w, _) in enumerate(lat_keys(d)):
                        m = pe.matmul(ps[:, ML_DEN[j % 2], a:a + w], ones, ml_pt[:, j % 2, n, 0:w], start=(n == 0),
                                      stop=(n == 3), skip_group_check=True)
                    m.then_inc(ml_values_ready, 1)
                    if d == 1 and h < 3:
                        scores(h + 1)
                    if j + 2 < len(ml_steps):
                        to_all(j + 2, 1, ML_ROWS, 0).then_inc(ml_rows_ready, 1)
                for h in range(4):
                    pe.wait_ge(ml_values_read, min(2 * h + 3 if h == 2 else 2 * h + 2, 8))
                    for v in range(2):
                        m = pe.matmul(ps[:, ML_SUM[h], 0:T], ones, ml_h[:, 2 * h + v, :], start=(v == 0), stop=(v == 1))
                    mine.did(m)
                for h in range(4):
                    from_act.expect()
                    for v in range(2):
                        m = pe.matmul(ps[:, ML_SQ[h], 0:T], ones, ml_sq(h, v), start=(v == 0),
                                      stop=(v == 1))
                    mine.did(m)

            pe.wait_ge(inputs_landed, 48)
            for k, s in enumerate(stages):
                if s.mods == 0:
                    from_dve.expect()
                opnd.n = operands_before[k] + FRESH[s.name]
                if s.name == "mla_uq":
                    pe.wait_ge(operand_ready, operands_before[k] + 5)
                    for n in range(2):
                        sums.expect()
                        ones_sum(4 + n, ma_acc[:, n, :], T)
                elif s.name == "att_out":
                    pe.wait_ge(operand_ready, opnd.n)
                run(k)
                if s.name == "mla_ukv":
                    pe.wait_ge(mod_read, 1)
                    pe.wait_ge(read_dve, freed[first_out[k] + 15][1])
                    transposes(ma_v, HEADS, 2, HEADS)
                    head_norms(mla_norms(), T)
                    ropes(mla_ropes)
                    attention(mla_units(), mla_groups())
                elif s.name == "att_in":
                    pe.wait_ge(read_dve, freed[first_out[k] + 11][1])
                    transposes(ga_v, 2, 4, 2)
                    head_norms(gqa_norms(), T2)
                    ropes(gqa_ropes)
                    attention(gqa_units(), gqa_groups())
                elif s.name == "ml_in":
                    pe.wait_ge(read_dve, freed[first_out[k] + 16][1])
                    transposes(ml_v, KD, 4, KD)
                    mlstm()
                elif s.name in ("ffn_out_2", "att_out", "ml_out"):
                    layer_norm_sums(s.width)

        @block.vector
        def _(dve):
            step = Tally(dve, dve_step)
            opnd = Tally(dve, operand_ready)
            sums = Tally(dve, sums_ready)
            stat = Tally(dve, stat_ready)
            std = Tally(dve, std_ready)
            silus = Tally(dve, silu_ready)
            to_pe, from_pe = Tally(dve, dve_ready), Tally(dve, pe_ready)
            to_act, from_act = Tally(dve, for_act), Tally(dve, for_dve)
            head_sq, head_sq_used = Tally(dve, head_squares), Tally(dve, head_squares_used)
            region_done = Tally(dve, region_free)
            tallies = dict(step=step, opnd=opnd, silus=silus)
            link = step.link
            cnt = dict(u=0, g=0)
            split_to = [0]
            tt, ts, stt = dve.tensor_tensor, dve.tensor_scalar, dve.scalar_tensor_tensor

            def split(c, i=None, iterations=1, per=0):
                k, j = owner[c]
                n = len(stages[k].tiles_of(j)) * P
                slot = c % SLOTS
                dve.wait_ge(hi_split, linear(lambda x: x + 1, c, per, i, iterations))
                tt(w_lo[:, slot, 0:n], raw[:, slot, 0:n], w_hi[:, slot, 0:n].bitcast(F32),
                   ALU.subtract).then_inc(lo_split, 1)

            def split_ahead(k, o):
                last = min(first_chunk[k] + stages[k].chunk_of(o)[-1] + AHEAD, n_chunks - 1)
                while split_to[0] <= last:
                    split(split_to[0])
                    split_to[0] += 1

            def split_modulation(s, o, i=None):
                body, o = (o - 2) // 4, (o - 2) % 4
                if s.mods is None or not 0 <= body < MOD_BODIES:
                    return
                for j in MOD_AFTER[o]:
                    n = MOD_SLOTS * (s.mods + body) + j + 1
                    dve.wait_ge(mod_hi_split, n if i is None else n + i * MOD_SLOTS)
                    rows = slice(4 * j, 4 * j + 4)
                    tt(mod_w_lo[:, rows, :], mod_w[:, rows, T:T2], mod_w_hi[:, rows, :].bitcast(F32),
                       ALU.subtract).then_inc(mod_lo_split, 1)

            def arrived(k, o, i=None, iterations=1):
                g = first_out[k] + o
                dve.wait_ge(out_ready, linear(lambda x: x + 1, g, 4, i, iterations))
                s = stages[k]
                return ps[:, g % BANKS, 0:(s.cols[o] if s.cols else s.width)]

            def bank_read(k, o, ins, i=None, iterations=1):
                g = first_out[k] + o
                ins.then_inc(read_dve, 1)
                dve.wait_ge(read_dve, linear(lambda x: freed[x][1], g, 4, i, iterations))

            def next_operand(o, gain, first=False):
                from_act.expect()
                opnd.did(stt(x_lo[:, o, 0:T], res[:, o, 0:T], gain, x_hi[:, o, 0:T].bitcast(F32),
                             ALU.mult, ALU.subtract))
                from_act.expect()
                if o == 0:
                    ins = dve.tensor_copy(acc[:, 0:T], silu[:, 0, 0:T])
                else:
                    ins = tt(acc[:, 0:T], acc[:, 0:T], silu[:, o % 2, 0:T], ALU.add)
                if o == KD - 1:
                    sums.did(ins)
                elif first and o < KD - 2:
                    to_act.link(ins)
                else:
                    link(ins)

            def inverse_rms():
                std.expect()
                link(dve.reciprocal(rstd[:, 0:T], rstd[:, 0:T]))

            def to_operand(hi, lo, src):
                link(dve.tensor_copy(hi, src))
                opnd.did(tt(lo, src, hi.bitcast(F32), ALU.subtract))

            def conv(dst, src, taps, width, bias=None, last=None):
                n = len(taps)
                for m, j in enumerate(reversed(range(n))):
                    if m == 0:
                        if bias is None:
                            ins = ts(dst, src(j), taps[j], None, ALU.mult)
                        else:
                            ins = ts(dst, src(j), taps[j], bias, ALU.mult, ALU.add)
                    else:
                        ins = stt(dst, src(j), taps[j], dst, ALU.mult, ALU.add)
                    (last if last and m == n - 1 else link)(ins)

            def gated(n):
                dve.wait_ge(gelu_ready, n + 1)
                opnd.need(opnd.n)
                link(tt(prod[:, 0:T], lr_g[:, n, :], lr_r[:, n, :], ALU.mult))
                to_operand(lr_o_hi[:, n, :], lr_o_lo[:, n, :], prod[:, 0:T])

            def read_out(k, o, layer, i=None, iterations=1):
                s = stages[k]
                name = s.name
                bank = arrived(k, o, i, iterations)
                done_with = lambda ins: bank_read(k, o, ins, i, iterations)
                r = rstd[:, 0:T]
                if name == "conv_c":
                    done_with(tt(cv_c[:, o, :], bank, r, ALU.mult))
                elif name == "conv_h":
                    done_with(tt(up[:], bank, r, ALU.mult))
                    link(tt(cv_x[:, o, 2:], up[:], cv_c[:, o, :], ALU.mult))
                    taps = [param("conv_w", ((layer // 3) * KD + o) * 3 + j) for j in range(3)]
                    conv(cv_y[:, o, :], lambda j: cv_x[:, o, j:j + T], taps, T)
                elif name == "conv_b":
                    done_with(tt(up[:], bank, r, ALU.mult))
                    link(tt(prod[:, 0:T], up[:], cv_y[:, o, :], ALU.mult))
                    to_operand(cv_hi[:, o, :], cv_lo[:, o, :], prod[:, 0:T])
                elif name == "lru_rec":
                    pad = lr_pad[:, o % 2, :]
                    done_with(tt(pad[:, 3:], bank, r, ALU.mult))
                    taps = [param("lru_conv_w", o * 4 + j) for j in range(4)]
                    conv(lr_rec[:, o, :], lambda j: pad[:, j:j + T], taps, T, bias=param("lru_conv_b", o))
                    to_operand(lr_rec_hi[:, o, :], lr_rec_lo[:, o, :], lr_rec[:, o, :])
                elif name == "lru_gate":
                    done_with(tt(lr_g[:, o, :], bank, r, ALU.mult))
                    from_act.expect()
                    link(tt(lr_t[:, o, :], lr_t[:, o, :], lr_i[:, o, :], ALU.mult))
                    link(dve.tensor_tensor_scan(lr_r[:, o, :], lr_a[:, o, :], lr_t[:, o, :], 0.0, ALU.mult, ALU.add))
                    if o >= 1:
                        gated(o - 1)
                elif name == "mla_down":
                    if o == 5:
                        done_with(tt(ma_k[:, 8, :], bank, r, ALU.mult))
                        return
                    done_with(tt(up[:], bank, r, ALU.mult))
                    n, first = (0, 0) if o < 3 else (1, 3)
                    if o == first:
                        link(tt(ma_acc[:, n, :], up[:], up[:], ALU.mult))
                    else:
                        link(tt(prod[:, 0:T], up[:], up[:], ALU.mult))
                        (sums.did if o in (2, 4) else link)(
                            tt(ma_acc[:, n, :], ma_acc[:, n, :], prod[:, 0:T], ALU.add))
                    gain = param("q_norm", o) if o < 3 else param("kv_norm", o - 3)
                    link(ts(scaled[:, 0, :], up[:], gain, None, ALU.mult))
                    to_operand(ma_x_hi[:, o, :], ma_x_lo[:, o, :], scaled[:, 0, :])
                elif name == "mla_uq":
                    done_with(tt(ma_q[:, o, :], bank, ma_rs[:, 0, :], ALU.mult))
                elif name == "mla_ukv":
                    dst = ma_k[:, o, :] if o < 8 else ma_v[:, o - 8, :]
                    done_with(tt(dst, bank, ma_rs[:, 1, :], ALU.mult))
                elif name == "ffn_in":
                    n = o // 2
                    if o % 2 == 0:
                        done_with(tt(scaled[:, n % 2, :], bank, r, ALU.mult))
                        return
                    done_with(tt(up[:], bank, r, ALU.mult))
                    silus.expect()
                    link(tt(prod[:, 0:T], up[:], silu[:, n % 2, 0:T], ALU.mult))
                    t = n if i is None else n + i * 2
                    to_operand(h_hi[:, t, 0:T], h_lo[:, t, 0:T], prod[:, 0:T])
                elif name == "ffn_in_2":
                    n, w = o // 2, s.width
                    g = first_out[k] + o - 1
                    dve.wait_ge(read_act, linear(lambda x: freed[x][1], g, 4, i, iterations))
                    opnd.need(opnd.n)
                    done_with(tt(prod[:, 0:w], bank, silu[:, n % 2, 0:w], ALU.mult))
                    t = n if i is None else n + i * 2
                    to_operand(h_hi[:, t, 0:w], h_lo[:, t, 0:w], prod[:, 0:w])
                elif name in ("conv_out", "lru_out", "mla_out", "ffn_out"):
                    done_with(tt(res[:, o, 0:T], bank, res[:, o, 0:T], ALU.add))
                    if layer + 1 == DEPTH and name == "ffn_out":
                        modulated(o, 0, 0, T2)
                    elif name != "ffn_out":
                        next_operand(o, param("ffn_norm", layer * KD + o))
                    else:
                        next_operand(o, param("mix_norm", (layer + 1) * KD + o))
                elif name == "att_in":
                    dst = ga_q[:, o, :] if o < 8 else ga_k[:, o - 8, :] if o < 10 else ga_v[:, o - 10, :]
                    done_with(dve.tensor_copy(dst, bank))
                elif name == "ml_in":
                    if o == 0:
                        link(ts(ml_row[:, 0, :], bank[0:64, :], param("ml_bias_i", rows=64), None, ALU.add))
                        done_with(dve.tensor_copy(ml_row[:, 1, :], bank[64:P, :]))
                        link(ts(ml_row[:, 1, :], ml_row[:, 1, :], param("ml_bias_f", rows=64), None, ALU.add))
                    elif o < 9:
                        taps = [param("ml_conv_w", (o - 1) * 3 + j) for j in range(3)]
                        if o >= 3:
                            from_act.expect()
                        if o < 5:
                            done_with(dve.tensor_copy(ml_pad[:, 0, 1:T + 1], bank))
                            conv(ml_cv[:, o % 2, 0, :], lambda j: ml_pad[:, 0, j:j + T], taps, T,
                                 bias=param("ml_conv_b", o - 1), last=to_act.did)
                        else:
                            done_with(dve.tensor_copy(ml_pad[:, :, 1:T + 1], bank.rearrange("p (a t) -> p a t", a=2)))
                            conv(ml_cv[:, o % 2, :, :], lambda j: ml_pad[:, :, j:j + T], taps, T2,
                                 bias=param("ml_conv_b", o - 1), last=to_act.did)
                    else:
                        done_with(dve.tensor_copy(ml_v[:, o - 9, :], bank))
                        if o <= 10:
                            from_act.expect()
                        if o == 10:
                            ml_log_forget()
                        elif o == 13:
                            ml_decay_rows()

            def halves(width):
                return [(0, T, 0)] + ([(T, T2, 1)] if width == T2 else [])

            def delta(k, o, layer, pos):
                s = stages[k]
                bank = arrived(k, o)
                w = s.width
                hs = halves(w)
                for a, b, v in hs:
                    gate = mod[:, layer, (2 + 3 * pos) * KD + o, v:v + 1]
                    ins = stt(res[:, o, a:b], bank[:, a:b], gate, res[:, o, a:b], ALU.mult, ALU.add)
                    if b == w:
                        bank_read(k, o, ins)
                    else:
                        step.did(ins)
                step.need(step.n)
                if o == 0:
                    link(dve.tensor_copy(acc[:, 0:w], res[:, o, 0:w]))
                else:
                    ins = tt(acc[:, 0:w], acc[:, 0:w], res[:, o, 0:w], ALU.add)
                    (sums.did if o == KD - 1 else link)(ins)

            def v_tile(o):
                return prod if o % 2 == 0 else silu[:, 0, :]

            def modulated(o, layer, pos, width):
                if o >= 2:
                    opnd.need(opnd.n - 1)
                for a, b, v in halves(width):
                    shift = mod[:, layer, 3 * pos * KD + o, v:v + 1]
                    scale = mod[:, layer, (3 * pos + 1) * KD + o, v:v + 1]
                    step.did(ts(v_tile(o)[:, a:b], res[:, o, a:b], scale, shift, ALU.mult, ALU.add))
                step.need(step.n)
                from_act.expect()
                opnd.did(tt(x_lo[:, o, 0:width], v_tile(o)[:, 0:width], x_hi[:, o, 0:width].bitcast(F32),
                            ALU.subtract))

            def post_norm(layer, pos, w):
                stat.expect()
                link(ts(prod[:, 0:w], ps[:, 4, 0:w], 1.0 / D, None, ALU.mult))
                for o in range(KD):
                    to_act.did(tt(res[:, o, 0:w], res[:, o, 0:w], prod[:, 0:w], ALU.subtract))
                std.expect()
                link(dve.reciprocal(rstd[:, 0:w], rstd[:, 0:w]))

                last = layer == DEPTH_2 - 1 and pos == 2
                to, to_pos = layer + (pos == 2), (pos + 1) % 3
                base = opnd.n

                def scaled_tile(o):
                    if o >= 2:
                        opnd.need(base + o - 1)
                    for a, b, v in halves(w):
                        scale = mod[:, to, (3 * to_pos + 1) * KD + o, v:v + 1]
                        ins = stt(v_tile(o)[:, a:b], res[:, o, a:b], scale, rstd[:, a:b], ALU.mult, ALU.mult)
                    to_act.did(ins)

                def lower_part(o):
                    from_act.expect()
                    for a, b, v in halves(w):
                        shift = mod[:, to, 3 * to_pos * KD + o, v:v + 1]
                        ins = stt(x_lo[:, o, a:b], v_tile(o)[:, a:b], shift, x_hi[:, o, a:b].bitcast(F32),
                                  ALU.add, ALU.subtract)
                    opnd.did(ins)

                if not last:
                    scaled_tile(0)
                    for o in range(KD):
                        if o + 1 < KD:
                            scaled_tile(o + 1)
                        to_act.need(to_act.n - (o + 1 < KD))
                        lower_part(o)
                    opnd.need(opnd.n)
                for o in range(KD):
                    gain = param("ln_g", (layer * 3 + pos) * KD + o)
                    to_act.did(stt(res[:, o, 0:w], res[:, o, 0:w], gain, rstd[:, 0:w], ALU.mult, ALU.mult))
                if not last:
                    from_act.expect()

            def log_sigmoid(x, t, n):
                link(stt(t[0], x, -1.0, x, ALU.mult, ALU.max))
                to_act.did(ts(t[0], t[0], -1.0, None, ALU.mult))
                from_act.expect()
                to_act.did(ts(t[2], t[1], 1.0, None, ALU.add))
                from_act.expect()
                link(stt(t[1], t[2], -1.0, t[1], ALU.add, ALU.subtract))
                link(dve.reciprocal(t[2], t[2]))
                link(tt(t[1], t[1], t[2], ALU.mult))
                link(tt(t[0], t[0], t[1], ALU.subtract))
                link(stt(x, x, 0.0, t[0], ALU.min, ALU.subtract))

            def rope_tables():
                ang, turns, r = ma_ang[:, 0, :], ma_ang[:, 1, :], ma_ang[:, 2, :]
                link(dve.tensor_copy(r, ma_pos[:]))
                link(ts(ang, r, const("inv_freq"), None, ALU.mult))
                magic = 1.5 * 2.0 ** 23
                link(ts(turns, ang, 1.0 / (2 * math.pi), None, ALU.mult))
                link(ts(turns, turns, magic, None, ALU.add))
                link(ts(turns, turns, magic, None, ALU.subtract))
                c1, c2 = 6.28125, 0.0019350051879882812
                for part in (c1, c2, 2 * math.pi - c1 - c2):
                    link(stt(ang, turns, -part, ang, ALU.mult, ALU.add))
                link(ts(ang, ang, math.pi, -math.pi, ALU.min, ALU.max))
                link(stt(r, ang, -1.0, ang, ALU.mult, ALU.max))
                to_act.did(ts(r, r, -1.0, math.pi / 2, ALU.mult, ALU.add))
                from_act.expect()

            def head_norms(tiles, width):
                base = head_sq_used.n
                for n, (x, row, pair, gain, one) in enumerate(tiles):
                    if n >= 2:
                        head_sq_used.need(base + n - 1)
                    head_sq.did(tt(hn_sq[:, n % 2, 0:width], x, x, ALU.mult))
                head_sq_used.skip(len(tiles) - 1)
                std.expect()
                to_pe.did(dve.reciprocal(hn_rs[:, 0:width], hn_rs[:, 0:width]))
                for n, (x, row, pair, gain, one) in enumerate(tiles):
                    from_pe.expect()
                    to_pe.did(stt(x, x, gain, ps[:, 5 + n % 2, 0:width], ALU.mult, ALU.mult))

            def ropes(tiles, cos, sin):
                for n, x in enumerate(tiles):
                    step.did(tt(rp[:, 0, :], x, cos, ALU.mult))
                    from_pe.expect()
                    to_pe.did(tt(rp[:, 1, :], ps[:, 4 + n % 2, 0:T], sin, ALU.mult))
                    to_pe.need(to_pe.n)
                    step.need(step.n)
                    ins = tt(x, rp[:, 0, :], rp[:, 1, :], ALU.add)
                    (to_pe.did if n == len(tiles) - 1 else link)(ins)

            def attention(units, groups, scale, masked):
                u0, g0 = cnt["u"], cnt["g"]

                def maximum(u):
                    keys, mask = units[u][1], units[u][2]
                    m = so_m[:, u % RING, :]
                    dve.wait_ge(scores_ready, u0 + u + 1)
                    src = ps[:, SCORE_BANKS[u % RING], 0:keys]
                    if u >= RING:
                        dve.wait_ge(probs_ready, u0 + u - RING + 1)
                    if masked:
                        link(stt(so_s[:, u % RING, 0:keys], src, scale, mask, ALU.mult, ALU.add))
                        dve.tensor_reduce(m[:, 0:1], so_s[:, u % RING, 0:keys], AX.X, ALU.max,
                                          negate=True).then_inc(max_ready, 1)
                    else:
                        link(dve.tensor_reduce(m[:, 1:2], src, AX.X, ALU.max, negate=True))
                        ts(m[:, 0:1], m[:, 1:2], scale, None, ALU.mult).then_inc(max_ready, 1)

                def normalise(u):
                    keys = units[u][1]
                    dve.wait_ge(probs_ready, u0 + u + 1)
                    link(dve.reciprocal(so_m[:, u % RING, 3:4], so_m[:, u % RING, 2:3]))
                    p = so_p[:, u % RING, 0:keys]
                    ts(p, p, so_m[:, u % RING, 3:4], None, ALU.mult).then_inc(probs_scaled, 1)

                def result(g):
                    dve.wait_ge(pv_done, g0 + g + 1)
                    to_operand(groups[g][1], groups[g][2], ps[:, g % 2, 0:T])

                for u in range(RING - 1):
                    maximum(u)
                for u in range(len(units)):
                    normalise(u)
                    if u + RING - 1 < len(units):
                        maximum(u + RING - 1)
                    if u % 2 == 1 and u >= 3:
                        result(u // 2 - 1)
                result(len(groups) - 1)
                cnt["u"] += len(units)
                cnt["g"] += len(groups)

            def ml_log_forget():
                r = [ml_row[:, n, :] for n in range(5)]
                log_sigmoid(r[1], [r[2], r[3], r[4]], T2)
                link(dve.memset(r[3], 1.0))

            def ml_decay_rows():
                r = [ml_row[:, n, :] for n in range(5)]

                def scan(dst, src, initial, op):
                    for lo, rev in ((0, False), (32, True)):
                        rows = slice(lo, lo + 32)
                        first = initial
                        for a in (T, 0):
                            d, s_, one = dst[rows, a:a + T], src[rows, a:a + T], r[3][rows, a:a + T]
                            if rev:
                                d, s_, one = d[:, ::-1], s_[:, ::-1], one[:, ::-1]
                            link(dve.tensor_tensor_scan(d, one, s_, first, ALU.mult, op))
                            end = a if rev else a + T - 1
                            first = dst[rows, end:end + 1]

                scan(r[4], r[1], 0.0, ALU.add)
                to_pe.did(tt(r[2], r[0], r[4], ALU.subtract))
                to_pe.need(to_pe.n)
                scan(r[1], r[2], 0.0, ALU.max)
                to_act.did(tt(r[4][:, 0:T], r[4][:, 0:T], r[1][:, 0:T], ALU.add))

            def mlstm():
                from_act.expect()
                to_pe.did(ts(ml_q[:], ml_q[:], P ** -0.5, None, ALU.mult))
                from_pe.skip(len_transposes(4 * KD))
                from_pe.expect()
                to_pe.did(dve.tensor_copy(ml_col[:], ps[:, 4, 0:T].rearrange("p (t r) -> p t r", t=4)))
                to_pe.need(to_pe.n)

                def masked(j):
                    dve.wait_ge(ml_rows_ready, j + 1)
                    if j >= 2:
                        dve.wait_ge(ml_decays_ready, j - 1)
                    n = 0
                    for t, a, w, m in lat_keys(ml_steps[j][1])[2:]:
                        ins = tt(ml_msk[:, j % 2, n:n + w], ps[:, ML_ROWS[j % 2], a:a + w], ml_const[:, m:m + w],
                                 ALU.add)
                        n += w
                    ins.then_inc(ml_masked_ready, 1)

                def weights(j):
                    h, d = ml_steps[j]
                    dve.wait_ge(ml_scores_ready, h + 1)
                    dve.wait_ge(ml_decays_ready, j + 1)
                    if j >= 2:
                        dve.wait_ge(ml_values_ready, j - 1)
                    for n, (t, a, w, _) in enumerate(lat_keys(d)):
                        at_ = (t % 2) * T + a
                        ins = tt(ml_pt[:, j % 2, n, 0:w], ps[:, t // 2, at_:at_ + w], ml_e[:, j % 2, n, 0:w], ALU.mult)
                    ins.then_inc(ml_weights_ready, 1)

                def values(j):
                    h, d = ml_steps[j]
                    dve.wait_ge(ml_values_ready, j + 1)
                    den, inv = ml_den[:, 0, :], ml_den[:, 1, :]
                    link(dve.tensor_copy(den, ps[:, ML_DEN[j % 2], 0:T]))
                    link(stt(inv, den, -1.0, den, ALU.mult, ALU.max))
                    link(tt(inv, inv, ps[:, ML_DEN[j % 2], T:T2], ALU.max))
                    link(dve.reciprocal(inv, inv))
                    num = ps[:, ML_NUM[j % 2], :]
                    if d == 0:
                        step.did(tt(ml_h[:, 2 * h, :], num[:, 0:T], inv, ALU.mult))
                        tt(ml_h[:, 2 * h + 1, :], num[:, T:T2], inv, ALU.mult).then_inc(ml_values_read, 1)
                    else:
                        step.did(tt(den, num[:, 0:T], inv, ALU.mult))
                        step.did(tt(inv, num[:, T:T2], inv, ALU.mult))
                        dve.wait_ge(ml_values_read, j)
                        step.need(step.n)
                        step.did(tt(ml_h[:, 2 * h, :], ml_h[:, 2 * h, :], den, ALU.add))
                        tt(ml_h[:, 2 * h + 1, :], ml_h[:, 2 * h + 1, :], inv, ALU.add).then_inc(ml_values_read, 1)
                    dve.wait_ge(ml_values_read, j + 1)

                masked(0)
                for j in range(len(ml_steps)):
                    if j + 1 < len(ml_steps):
                        masked(j + 1)
                    weights(j)
                    if j >= 1:
                        values(j - 1)
                values(len(ml_steps) - 1)
                for h in range(4):
                    from_pe.expect()
                    link(ts(ml_den[:, 0, :], ps[:, ML_SUM[h], 0:T], 1.0 / (2 * P), None, ALU.mult))
                    for v in range(2):
                        x = ml_h[:, 2 * h + v, :]
                        ins = tt(x, x, ml_den[:, 0, :], ALU.subtract)
                        (to_act.did if v else step.did)(ins)
                    to_act.need(to_act.n)
                from_pe.skip(4)
                for h in range(4):
                    from_act.expect()
                    link(dve.reciprocal(ml_q[:, h, :], ml_q[:, h, :]))
                    for v in range(2):
                        n = 2 * h + v
                        x = ml_h[:, n, :]
                        link(tt(x, x, ml_q[:, h, :], ALU.mult))
                        link(stt(x, x, param("ml_norm_g", n), ml_og[:, n, :], ALU.mult, ALU.mult))
                        to_operand(x_hi[:, n, 0:T], x_lo[:, n, 0:T], x)

            def run(k, layer, pos):
                s = stages[k]
                count = sum(bodies(k, AHEAD)[:2]) if s.name in ("ffn_in", "ffn_in_2") else 0
                if s.mods is not None:
                    count = MOD_BODIES
                def one(o, i=None, iterations=1):
                    if s.readers[o] == "act":
                        return
                    if s.name in ("ffn_out_2", "att_out", "ml_out"):
                        delta(k, o, layer, pos)
                    else:
                        read_out(k, o, layer, i, iterations)
                o = 0
                if count:
                    split_ahead(k, 0)
                    assert split_to[0] == first_chunk[k] + AHEAD + 1
                    one(0)
                    split_ahead(k, 1)
                    one(1)
                    split_modulation(s, 1)
                    split_ahead(k, 2)
                    one(2)
                    split_modulation(s, 2)
                    split_ahead(k, 3)
                    one(3)
                    split_modulation(s, 3)
                    counts = dict(step=4, opnd=2, silus=2) if s.name == "ffn_in" else dict(step=2, opnd=2, silus=0)
                    with dve.Fori(0, count - 1) as i:
                        for name, t in tallies.items():
                            t.enter(i, counts[name])
                        for o in range(4, 8):
                            if s.name == "ffn_in":
                                one(o, i, count - 1)
                                split(first_chunk[k] + o + AHEAD, i, count - 1, 4)
                            else:
                                split(first_chunk[k] + o + AHEAD, i, count - 1, 4)
                                one(o, i, count - 1)
                            split_modulation(s, o, i)
                        for t in tallies.values():
                            t.leave(count - 1)
                    split_to[0] += 4 * (count - 1)
                    o = 4 * count
                for o in range(o, s.outs):
                    if len(s.chunk_of(o)) == 1 and s.name != "ml_in":
                        one(o)
                        split_ahead(k, o)
                    else:
                        split_ahead(k, o)
                        one(o)
                    split_modulation(s, o)

            def modulation(m):
                dve.wait_ge(mod_turned, (m + 1) * MOD_GROUPS // DEPTH_2)
                a = PARAM_AT["ada_b"] + 72 * m
                tt(mod[:, m], ps[:, 7, 0:144].rearrange("p (n v) -> p n v", v=2),
                   par[:, a:a + 72].unsqueeze(2).to_broadcast([P, 72, 2]), ALU.add).then_inc(mod_read, 1)
                dve.wait_ge(mod_read, m + 1)
                for q in range(3):
                    x = mod[:, m, (3 * q + 1) * KD:(3 * q + 2) * KD, :]
                    link(ts(x, x, 1.0, None, ALU.add))
                    if q != 1:
                        x = mod[:, m, (3 * q + 2) * KD:(3 * q + 3) * KD, :]
                        link(ts(x, x, 0.5, None, ALU.mult))
                for q in range(3):
                    norm = 3 * m + q - 1
                    if norm < 0:
                        continue
                    shift, scale = mod[:, m, 3 * q * KD:(3 * q + 1) * KD, :], mod[:, m, (3 * q + 1) * KD:(3 * q + 2) * KD, :]
                    g, b = (par[:, PARAM_AT[p] + norm * KD:PARAM_AT[p] + (norm + 1) * KD].unsqueeze(2)
                            .to_broadcast([P, KD, 2]) for p in ("ln_g", "ln_b"))
                    t = up[:, 0:2 * KD].rearrange("p (n v) -> p n v", v=2)
                    link(tt(t, scale, b, ALU.mult))
                    link(tt(shift, shift, t, ALU.add))
                    link(tt(scale, scale, g, ALU.mult))

            def len_transposes(n):
                return n // 4

            def decay_constants():
                lam = decay_c[:, 3, :]
                link(dve.tensor_copy(lam, par[:, PARAM_AT["lam"]:PARAM_AT["lam"] + KL]))
                log_sigmoid(lam, [decay_c[:, n, :] for n in range(3)], KL)
                link(ts(decay_c[:, 4, :], lam, 8.0, None, ALU.mult))
                to_act.did(ts(decay_c[:, 5, :], lam, -8.0, None, ALU.mult))

            dve.wait_ge(inputs_landed, 48)
            for o in range(KD):
                next_operand(o, param("mix_norm", o), first=True)
                if o in FIRST_SPLITS:
                    split(split_to[0])
                    split_to[0] += 1
            from_act.expect()
            to_pe.did(tt(cond_parts[:, :, 2:4], cond[:], cond_parts[:, :, 0:2].bitcast(F32), ALU.subtract))
            layer, pos = 0, 0
            for k, s in enumerate(stages):
                name = s.name
                if name in ("conv_c", "lru_rec", "mla_down", "ffn_in"):
                    stat.skip()
                    split_ahead(k, 0)
                    inverse_rms()
                if name == "ffn_out":
                    if layer == 0:
                        decay_constants()
                    if layer % 2 == 1:
                        modulation(layer // 2)
                        if layer == DEPTH - 1:
                            for p in ("ln_g", "ln_b"):
                                x = par[:, PARAM_AT[p]:PARAM_AT[p] + (3 * DEPTH_2 - 1) * KD]
                                ins = ts(x, x, ALPHA, None, ALU.mult)
                                (link if p == "ln_g" else to_act.link)(ins)
                if name == "conv_c":
                    link(dve.memset(cv_x[:, :, 0:2], 0.0))
                elif name == "lru_rec":
                    link(dve.memset(lr_pad[:, :, 0:3], 0.0))
                elif name == "lru_gate":
                    for n in range(KL):
                        from_act.expect()
                        step.did(tt(prod[:, 0:T], lr_a[:, n, :], lr_a[:, n, :], ALU.mult))
                        step.did(tt(lr_i[:, n, :], lr_i[:, n, :], lr_rec[:, n, :], ALU.mult))
                        step.need(step.n)
                        to_act.did(stt(lr_t[:, n, :], prod[:, 0:T], 1.0, lr_t[:, n, :], ALU.add, ALU.mult))
                        to_act.need(to_act.n)
                        if n == KL // 2 - 1:
                            split_ahead(k, 0)
                    split_ahead(k, 1)
                elif name == "mla_down":
                    region_done.did(dve.memset(ma_ang[:, 0, 0:1], 0.0))
                    region_done.need(region_done.n)
                elif name == "mla_uq":
                    stat.skip(2)
                    for n in range(2):
                        std.expect()
                        link(dve.reciprocal(ma_rs[:, n, :], ma_rs[:, n, :]))
                    dve.wait_ge(consts_landed, 48)
                    rope_tables()
                elif name == "att_in":
                    region_done.did(dve.memset(hn_rs[:, 0:1], 0.0))
                    region_done.need(region_done.n)
                elif name == "ml_in":
                    region_done.did(dve.memset(ml_pad[:], 0.0))
                    region_done.need(region_done.n)
                run(k, layer, pos)
                if name == "lru_gate":
                    gated(KL - 1)
                elif name == "mla_ukv":
                    from_pe.skip(len_transposes(2 * HEADS))
                    stat.skip()
                    head_norms(mla_norms(), T)
                    ropes(mla_ropes, ma_cos[:], ma_sin[:])
                    attention(mla_units(), mla_groups(), (NOPE + ROPE) ** -0.5, True)
                elif name == "att_in":
                    from_pe.skip(len_transposes(8))
                    stat.skip()
                    head_norms(gqa_norms(), T2)
                    dve.wait_ge(consts_landed, 64)
                    ropes(gqa_ropes, ga_rope[:, 0, :], ga_rope[:, 1, :])
                    attention(gqa_units(), gqa_groups(), P ** -0.5, False)
                elif name == "ml_in":
                    dve.wait_ge(consts_landed, 80)
                    mlstm()
                if name == "ffn_out":
                    layer += 1
                    if layer == DEPTH:
                        from_act.expect()
                        layer = 0
                elif name in ("ffn_out_2", "att_out", "ml_out"):
                    post_norm(layer, pos, s.width)
                    layer, pos = (layer + 1, 0) if pos == 2 else (layer, pos + 1)

        @block.scalar
        def _(act):
            step = Tally(act, act_step)
            stat = Tally(act, stat_ready)
            std = Tally(act, std_ready)
            silus = Tally(act, silu_ready)
            to_pe, from_pe = Tally(act, act_ready), Tally(act, pe_ready)
            from_dve, to_dve = Tally(act, for_act), Tally(act, for_dve)
            sq, sq_used = Tally(act, squares_ready), Tally(act, squares_used)
            tallies = dict(silus=silus)
            cnt = dict(u=0, g=0)
            split_to = [0]
            f = act.activation

            def split(c, i=None, iterations=1, per=0):
                k, j = owner[c]
                n = len(stages[k].tiles_of(j)) * P
                slot = c % SLOTS
                v = 16 * (c // SLOTS + 1)
                act.wait_ge(landed[slot], v if i is None else v + i * (16 * (per // SLOTS)))
                before = c - SLOTS
                if before >= 0:
                    v = linear(lambda x: done[x][1], before, per, i, iterations)
                    act.wait_ge(out_ready if done[before][0] == "out" else part_used, v)
                f(w_hi[:, slot, 0:n], raw[:, slot, 0:n], ACT.Copy).then_inc(hi_split, 1)

            def split_ahead(k, o):
                last = min(first_chunk[k] + stages[k].chunk_of(o)[-1] + AHEAD, n_chunks - 1)
                while split_to[0] <= last:
                    split(split_to[0])
                    split_to[0] += 1

            def mod_load(g, j, i=None):
                if g > 0:
                    n = MOD_SLOTS * (g - 1) + j + 1
                    act.wait_ge(mod_lo_split, n if i is None else n + i * MOD_SLOTS)
                src = MOD_SLOTS * g + j
                src = dram["w_ada"][src if i is None else src + i * MOD_SLOTS]
                act.dma_start(mod_w[:, 4 * j:4 * j + 4, T:T2],
                              src.rearrange("p (a b) -> p a b", b=T)).then_inc(mod_landed[j], 16)

            def mod_split(g, j, i=None):
                act.wait_ge(mod_landed[j], 16 * (g + 1) if i is None else 16 * (g + 1) + i * 16)
                if g > 0:
                    n = MOD_SLOTS * (g - 1) + j + 1
                    act.wait_ge(mod_used, n if i is None else n + i * MOD_SLOTS)
                rows = slice(4 * j, 4 * j + 4)
                f(mod_w_hi[:, rows, :], mod_w[:, rows, T:T2], ACT.Copy).then_inc(mod_hi_split, 1)

            def modulation(s, o, i=None):
                if s.mods is None:
                    return
                body, o = o // 4, o % 4
                if o == 3 and 1 <= body <= MOD_BODIES:
                    g = s.mods + body - 1
                    n = MOD_SLOTS * (g + 1)
                    act.wait_ge(mod_used, n if i is None else n + i * MOD_SLOTS)
                    f(mod_rows, ps[0:4, 6, :].rearrange("p (a b) -> p a b", b=T),
                      ACT.Copy).then_inc(mod_rows_copied, 1)
                if 0 <= (4 * body + o - 3) // 4 < MOD_BODIES:
                    g = s.mods + (4 * body + o - 3) // 4
                    if g + 1 < MOD_GROUPS:
                        for j in MOD_AFTER[(o - 3) % 4]:
                            mod_load(g + 1, j, i)
                if body < MOD_BODIES and o >= 1:
                    for j in MOD_AFTER[o - 1]:
                        mod_split(s.mods + body, j, i)

            def deviation(dst, src, n, eps):
                stat.expect()
                std.did(f(dst, src, ACT.Sqrt, bias=eps, scale=1.0 / n))

            def next_operand(o, gain):
                to_dve.did(f(x_hi[:, o, 0:T], res[:, o, 0:T], ACT.Identity, scale=gain))
                to_dve.did(f(silu[:, o % 2, 0:T], res[:, o, 0:T], ACT.Square))

            def modulated(o, layer, pos, w):
                for a, b, v in ((0, T, 0), (T, T2, 1))[:w // T]:
                    ins = f(x_hi[:, o, a:b], res[:, o, a:b], ACT.Identity,
                            bias=mod[:, layer, 3 * pos * KD + o, v:v + 1],
                            scale=mod[:, layer, (3 * pos + 1) * KD + o, v:v + 1])
                to_dve.did(ins)

            def times_alpha(k, o):
                act.wait_ge(operand_ready, operands_before[k + 1] + o + 1)
                return f(res[:, o, :], res[:, o, :], ACT.Copy, scale=ALPHA)

            def read_out(k, o, i=None, iterations=1, layer=0):
                s = stages[k]
                name = s.name
                g = first_out[k] + o
                if name == "ffn_in" and o % 2 == 0:
                    n = o // 2
                    act.wait_ge(read_dve, linear(lambda x: freed[x][1], g, 4, i, iterations))
                    silus.did(f(silu[:, n % 2, 0:T], scaled[:, n % 2, :], ACT.Silu))
                elif name in ("conv_out", "lru_out", "mla_out", "ffn_out"):
                    act.wait_ge(read_dve, freed[g][1])
                    if name != "ffn_out":
                        next_operand(o, param("ffn_norm", layer * KD + o))
                    elif layer + 1 < DEPTH:
                        next_operand(o, param("mix_norm", (layer + 1) * KD + o))
                    else:
                        modulated(o, 0, 0, T2)
                        if o >= 1:
                            times_alpha(k, o - 1)
                        if o == KD - 1:
                            to_dve.did(times_alpha(k, o))
                elif name == "lru_gate":
                    act.wait_ge(read_dve, freed[g][1])
                    f(lr_g[:, o, :], lr_g[:, o, :], ACT.Gelu_apprx_tanh).then_inc(gelu_ready, 1)
                elif name == "ml_in" and 1 <= o < 9:
                    from_dve.expect()
                    if o < 5:
                        to_dve.did(f(ml_q[:, o - 1, :], ml_cv[:, o % 2, 0, :], ACT.Silu))
                    else:
                        to_dve.did(f(ml_k[:, o - 5, :], ml_cv[:, o % 2, :, :].rearrange("p a t -> p (a t)"), ACT.Silu))
                elif name == "ml_in" and o in (10, 13):
                    r = [ml_row[:, n, :] for n in range(5)]
                    if o == 10:
                        log_sigmoid([r[2], r[3], r[4]])
                    else:
                        from_dve.expect()
                        to_dve.did(f(r[4][:, 0:T], r[4][:, 0:T], ACT.Exp, scale=-1.0))
                elif s.readers[o] == "act":
                    act.wait_ge(out_ready, linear(lambda x: x + 1, g, 4, i, iterations))
                    bank = ps[:, g % BANKS, 0:(s.cols[o] if s.cols else s.width)]
                    if name == "lru_gates":
                        n = o // 2
                        if o % 2 == 0:
                            ins = f(lr_r[:, n, :], bank, ACT.Sigmoid, bias=param("gate_a_b", n))
                        else:
                            ins = f(lr_i[:, n, :], bank, ACT.Sigmoid, bias=param("gate_x_b", n))
                    elif name == "ffn_in_2":
                        n = o // 2
                        if n >= 2 or i is not None:
                            act.wait_ge(read_dve, linear(lambda x: freed[x][1], g - 3, 4, i, iterations))
                        ins = f(silu[:, n % 2, 0:s.width], bank, ACT.Silu)
                    else:
                        ins = f(ml_og[:, o - 17, :], bank, ACT.Sigmoid)
                    ins.then_inc(read_act, 1)

            def layer_norm(k, w, layer, pos):
                stat.skip()
                for o in range(KD):
                    from_dve.expect()
                    sq.did(f(squares[:, o, 0:w], res[:, o, 0:w], ACT.Square))
                sq_used.expect()
                std.did(f(rstd[:, 0:w], ps[:, 5, 0:w], ACT.Sqrt, bias=const("eps_ln"), scale=1.0 / D))
                last = layer == DEPTH_2 - 1 and pos == 2

                if not last:
                    to, to_pos = layer + (pos == 2), (pos + 1) % 3
                    for o in range(KD):
                        from_dve.expect()
                        v_tile = prod if o % 2 == 0 else silu[:, 0, :]
                        for a, b, v in ((0, T, 0), (T, T2, 1))[:w // T]:
                            ins = f(x_hi[:, o, a:b], v_tile[:, a:b], ACT.Identity,
                                    bias=mod[:, to, 3 * to_pos * KD + o, v:v + 1])
                        to_dve.did(ins)
                for o in range(KD):
                    from_dve.expect()
                    ins = f(res[:, o, 0:w], res[:, o, 0:w], ACT.Identity,
                            bias=param("ln_b", (layer * 3 + pos) * KD + o))
                    if last:
                        ins.then_inc(result_ready, 1)
                    elif o == KD - 1:
                        to_dve.did(ins)

            def log_sigmoid(t):
                from_dve.expect()
                to_dve.did(f(t[1], t[0], ACT.Exp))
                from_dve.expect()
                to_dve.did(f(t[0], t[2], ACT.Ln))

            def transposes(dst, jobs):
                for n in range(jobs // 4):
                    from_pe.expect()
                    to_pe.did(f(dst[:, n * 512:n * 512 + 512], ps[:, 6 + n % 2, :], ACT.Copy))

            def head_norms(n, width):
                stat.expect()
                std.did(f(hn_rs[:, 0:width], ps[0:32, 4, 0:width], ACT.Sqrt, bias=const("eps", rows=32),
                          scale=const("row_scale", rows=32)))
                from_pe.skip(n)

            def attention(units, groups, scale, masked):
                u0, g0 = cnt["u"], cnt["g"]

                def weights(u):
                    keys = units[u][1]
                    m = so_m[:, u % RING, :]
                    act.wait_ge(max_ready, u0 + u + 1)
                    if u >= RING:
                        act.wait_ge(transposed, u0 + u - RING + 1)
                    src = so_s[:, u % RING, 0:keys] if masked else ps[:, SCORE_BANKS[u % RING], 0:keys]
                    f(so_p[:, u % RING, 0:keys], src, ACT.Exp, bias=m[:, 0:1], scale=1.0 if masked else scale,
                      accum_out=m[:, 2:3]).then_inc(probs_ready, 1)

                def turn(u):
                    keys, g = units[u][1], u // 2
                    act.wait_ge(transposed, u0 + u + 1)
                    if g >= 2:
                        act.wait_ge(pv_done, g0 + g - 1)
                    a = (u % 2) * P
                    f(so_pt[:, g % 2, 0:keys // P, a:a + P],
                      ps[:, 6 + u % 2, 0:keys].rearrange("p (k q) -> p k q", q=P), ACT.Copy).then_inc(turned, 1)

                for u in range(RING - 1):
                    weights(u)
                for u in range(len(units)):
                    if u + RING - 1 < len(units):
                        weights(u + RING - 1)
                    turn(u)
                cnt["u"] += len(units)
                cnt["g"] += len(groups)

            def mlstm():
                from_pe.skip(1)
                for j, (h, d) in enumerate(ml_steps):
                    act.wait_ge(ml_masked_ready, j + 1)
                    if j >= 2:
                        act.wait_ge(ml_weights_ready, j - 1)
                    n_at, col = 0, 32 * d + h
                    for n, (t, a, w, m) in enumerate(lat_keys(d)):
                        if m is None:
                            src = ps[:, ML_ROWS[j % 2], 0:T]
                        else:
                            src, n_at = ml_msk[:, j % 2, n_at:n_at + w], n_at + w
                        ins = f(ml_e[:, j % 2, n, 0:w], src, ACT.Exp, bias=ml_col[:, t, col:col + 1], scale=-1.0)
                    ins.then_inc(ml_decays_ready, 1)
                from_pe.skip(4)
                for h in range(4):
                    from_dve.expect()
                    for v in range(2):
                        ins = f(ml_sq(h, v), ml_h[:, 2 * h + v, :], ACT.Square)
                    to_pe.did(ins)
                for h in range(4):
                    from_pe.expect()
                    to_dve.did(f(ml_q[:, h, :], ps[:, ML_SQ[h], 0:T], ACT.Sqrt, bias=const("eps_ln"), scale=0.5 / P))

            def run(k, layer):
                s = stages[k]
                count = sum(bodies(k, AHEAD)[:2]) if s.name in ("ffn_in", "ffn_in_2") else 0
                if s.mods is not None:
                    count = MOD_BODIES - 1
                o = 0
                if count:
                    for o in range(4):
                        split_ahead(k, o)
                        read_out(k, o)
                        modulation(s, o)
                    with act.Fori(0, count - 1) as i:
                        silus.enter(i, 2 if s.name == "ffn_in" else 0)
                        for o in range(4, 8):
                            split(first_chunk[k] + o + AHEAD, i, count - 1, 4)
                            read_out(k, o, i, count - 1)
                            modulation(s, o, i)
                        silus.leave(count - 1)
                    split_to[0] += 4 * (count - 1)
                    o = 4 * count
                for o in range(o, s.outs):
                    split_ahead(k, o)
                    read_out(k, o, layer=layer)
                    modulation(s, o)

            act.wait_ge(inputs_landed, 48)
            for o in range(KD):
                if o >= 2:
                    from_dve.expect()
                next_operand(o, param("mix_norm", o))
                if o in FIRST_SPLITS:
                    split(split_to[0])
                    split_to[0] += 1
            for j in range(MOD_SLOTS):
                mod_load(0, j)
            a = PARAM_AT["cond"]
            step.link(f(cond[:], par[:, a:a + 2 * KD].rearrange("p (k v) -> p k v", v=2), ACT.Silu))
            to_dve.did(f(cond_parts[:, :, 0:2], cond[:], ACT.Copy))
            layer, pos = 0, 0
            for k, s in enumerate(stages):
                name = s.name
                if name == "ffn_out":
                    if layer == 0:
                        log_sigmoid([decay_c[:, n, :] for n in range(3)])
                        from_dve.expect()
                    elif layer == DEPTH - 1:
                        from_dve.expect()
                        act.wait_ge(consts_landed, 48)
                if name in ("conv_c", "lru_rec", "mla_down", "ffn_in"):
                    split_ahead(k, 0)
                    deviation(rstd[:, 0:T], ps[:, 4, 0:T], D, const("eps"))
                elif name == "mla_uq":
                    deviation(ma_rs[:, 0, :], ps[:, 4, 0:T], Q_RANK, const("eps"))
                    deviation(ma_rs[:, 1, :], ps[:, 5, 0:T], KV_RANK, const("eps"))
                    from_dve.expect()
                    f(ma_sin[:], ma_ang[:, 0, :], ACT.Sin)
                    to_dve.did(f(ma_cos[:], ma_ang[:, 2, :], ACT.Sin))
                run(k, layer)
                if name == "lru_gates":
                    act.wait_ge(read_act, freed[first_out[k] + s.outs - 1][1])
                    for n in range(KL):
                        f(lr_a[:, n, :], lr_r[:, n, :], ACT.Exp, scale=decay_c[:, 4, n:n + 1])
                        to_dve.did(f(lr_t[:, n, :], lr_r[:, n, :], ACT.Tanh, scale=decay_c[:, 5, n:n + 1]))
                        if n == KL // 2 - 1:
                            split_ahead(k + 1, 0)
                    for n in range(KL):
                        from_dve.expect()
                        to_dve.did(f(lr_t[:, n, :], lr_t[:, n, :], ACT.Sqrt))
                        if n in (1, 6):
                            split_ahead(k + 1, 1 + n // 6)
                elif name == "mla_ukv":
                    transposes(ma_vt[:].rearrange("p a b -> p (a b)"), 2 * HEADS)
                    head_norms(len(mla_norms()), T)
                    from_pe.skip(len(mla_ropes))
                    attention(mla_units(), mla_groups(), (NOPE + ROPE) ** -0.5, True)
                elif name == "att_in":
                    transposes(ga_vt[:].rearrange("p a b -> p (a b)"), 8)
                    head_norms(len(gqa_norms()), T2)
                    from_pe.skip(len(gqa_ropes))
                    attention(gqa_units(), gqa_groups(), P ** -0.5, False)
                elif name == "ml_in":
                    transposes(ml_vt[:].rearrange("p a b -> p (a b)"), 4 * KD)
                    mlstm()
                elif name == "ffn_out":
                    layer = (layer + 1) % DEPTH
                elif name in ("ffn_out_2", "att_out", "ml_out"):
                    layer_norm(k, s.width, layer, pos)
                    layer, pos = (layer + 1, 0) if pos == 2 else (layer, pos + 1)


def tiles(w):
    k, n = w.shape
    return w.reshape(k // P, P, n // P, P).transpose(2, 1, 0, 3).reshape(n // P, P, k)


def grouped(w, per):
    t = tiles(w)
    n, p, k = t.shape
    return t.reshape(n // per, per, p, k).transpose(0, 2, 1, 3).reshape(n // per, p, per * k)


def modulation_chunks(w):
    k, n = w.shape
    w = w.reshape(k // (2 * P), 2, P, n // MOD_WIDTH, MOD_WIDTH).transpose(3, 0, 2, 1, 4)
    return w.reshape(-1, P, 2 * MOD_WIDTH)


def by_feature(v):
    v = v.reshape(-1, v.shape[-1] // P, P)
    return v.transpose(2, 0, 1).reshape(P, -1)


def gate_up(w, ff):
    k = w.shape[0]
    return w.reshape(k, 2, ff // P, P).transpose(0, 2, 1, 3).reshape(k, 2 * ff)


def constants():
    c = np.zeros((P, N_CONST), np.float32)
    p = np.arange(P)

    def put(name, v):
        c[:, CONST_AT[name]:CONST_AT[name] + CONST_SIZES[name]] = v

    put("ident", np.eye(P))
    put("ones", 1.0)
    rot = np.zeros((P, P), np.float32)
    for m in range(P):
        if m % 64 < 32:
            rot[m + 32, m] = -1.0
        else:
            rot[m - 32, m] = 1.0
    put("rot", rot)
    z = np.zeros((P, 63), np.float32)
    z[:, 31] = 1.0
    put("sel", z)
    z = np.zeros((P, 64), np.float32)
    z[:64, 31] = 1.0
    z[64:, 32] = 1.0
    put("sel2", z)
    c[0:4, CONST_AT["fold"]:CONST_AT["fold"] + 2] = [[1, 0], [0, 1], [1, 0], [0, 1]]
    put("eps", NORM_EPS)
    put("eps_ln", LN_EPS)
    inv = (10000.0 ** (-np.arange(0, ROPE, 2, dtype=np.float32) / ROPE)).astype(np.float32)
    put("inv_freq", inv[p % 32][:, None])
    scale = np.where(p < 16, 1.0 / NOPE, 1.0 / ROPE).astype(np.float32)
    put("row_scale", scale[:, None])
    mla = np.zeros((P, N_MLA_CONST), np.float32)
    for n in range(5):
        mla[16 + 2 * n, n * P:n * P + 64] = 1.0
        mla[17 + 2 * n, n * P + 64:n * P + P] = 1.0
    q, key = p[:, None], p[None, :]
    mla[:, 6 * P:] = np.where(key <= q, 0.0, -BIG)
    ml = np.zeros((P, N_ML_CONST), np.float32)
    s, t = p[:, None], p[None, :]
    ml[:, 0:P] = np.where(s <= t, 0.0, BIG)
    ml[:, 2 * P:] = np.where(s >= t, 0.0, BIG)
    pos = np.arange(T)
    rope = np.zeros((P, 2, T), np.float32)
    inv = (10000.0 ** (-np.arange(32, dtype=np.float32) / 32)).astype(np.float32)
    for m in range(P):
        where = (pos // 64 if m < 64 else pos % 64).astype(np.float32)
        ang = where * inv[m % 32]
        rope[m, 0], rope[m, 1] = np.cos(ang), np.sin(ang)
    return c, mla, ml, rope


def _lay_out(a):
    f = {}
    cat = np.concatenate
    f["x"] = a["x"][0].T.reshape(KD, P, T).transpose(1, 0, 2)
    f["ctx"] = a["ctx_2"][0].T.reshape(KD, P, T).transpose(1, 0, 2)
    f["positions"] = a["positions"].reshape(1, T)
    f["w_conv_in"] = cat([tiles(w[:, n * D:(n + 1) * D]) for w in a["conv_w_in"] for n in (1, 2, 0)])
    f["w_conv_out"] = cat([tiles(w) for w in a["conv_w_out"]])
    w = a["lru_w_in"][0]
    f["w_lru_in"] = cat([tiles(w[:, LRU:]), tiles(w[:, :LRU])])
    gates = np.stack([a["lru_gate_a_w"][0], a["lru_gate_x_w"][0]], 1).reshape(2 * KL, P, P)
    f["w_lru_gates"] = gates.reshape(5, 4, P, P).transpose(0, 2, 1, 3).reshape(5, P, 4 * P)
    f["w_lru_out"] = tiles(a["lru_w_out"][0])
    w = a["mla_w_down"][0]
    f["w_mla_down"] = tiles(cat([w, w[:, Q_RANK + KV_RANK:]], axis=1))
    w = a["mla_w_uq"][0].reshape(Q_RANK, HEADS, NOPE + ROPE)
    w = cat([w[:, :, :NOPE].reshape(Q_RANK, -1), w[:, :, NOPE:].reshape(Q_RANK, -1)], axis=1)
    f["w_mla_uq"] = grouped(w, 2)
    w = a["mla_w_ukv"][0].reshape(KV_RANK, HEADS, 2, P)
    f["w_mla_ukv"] = grouped(w.transpose(0, 2, 1, 3).reshape(KV_RANK, -1), 4)
    f["w_mla_o"] = tiles(a["mla_w_o"][0])
    f["w_ffn_in"] = cat([tiles(gate_up(w, FF)) for w in a["ffn_w_gu"]])
    f["w_ffn_out"] = cat([tiles(w) for w in a["ffn_w_down"]])
    f["w_ada"] = cat([modulation_chunks(w) for w in a["ada_w_2"]])
    f["w_ffn_in_2"] = cat([tiles(gate_up(w, FF)) for l in a["ffn_w_in_2"] for w in l])
    f["w_ffn_out_2"] = cat([tiles(w) for l in a["ffn_w_out_2"] for w in l])
    f["w_att_in"] = tiles(a["att_w_in_2"][0])
    f["w_att_out"] = tiles(a["att_w_out_2"][0])
    w = a["ml_w_in_2"][0]
    g = w[:, 3072:].reshape(D, 4, 4)
    gt = np.zeros((D, P), np.float32)
    for kind, at in ((0, 0), (2, 32), (1, 64), (3, 96)):
        gt[:, at:at + 4] = g[:, kind]
    f["w_ml_in"] = tiles(cat([gt, w[:, :3072]], axis=1))
    f["w_ml_out"] = tiles(a["ml_w_out_2"][0])

    par = np.zeros((P, N_PARAM), np.float32)

    def put(name, v):
        par[:, PARAM_AT[name]:PARAM_AT[name] + PARAM_SIZES[name]] = v

    put("mix_norm", by_feature(a["mix_norm"]))
    put("ffn_norm", by_feature(a["ffn_norm"]))
    put("conv_w", a["conv_w"].reshape(2, 3, KD, P).transpose(3, 0, 2, 1).reshape(P, -1))
    put("lru_conv_w", a["lru_conv_w"].reshape(4, KL, P).transpose(2, 1, 0).reshape(P, -1))
    put("lru_conv_b", by_feature(a["lru_conv_b"]))
    put("gate_a_b", a["lru_gate_a_b"][0].T)
    put("gate_x_b", a["lru_gate_x_b"][0].T)
    put("lam", by_feature(a["lru_lambda"]))
    put("q_norm", by_feature(a["mla_q_norm"]))
    put("kv_norm", by_feature(a["mla_kv_norm"]))
    put("qn_norm", a["mla_qn_norm"].T)
    put("kn_norm", a["mla_kn_norm"].T)
    put("qr_norm", cat([a["mla_qr_norm"]] * 2, axis=1).T)
    put("kr_norm", cat([a["mla_kr_norm"]] * 2, axis=1).T)
    put("ada_b", by_feature(a["ada_b_2"]))
    put("ln_g", by_feature(a["ln_g_2"]))
    put("ln_b", by_feature(a["ln_b_2"]))
    put("att_q_gain", a["att_q_gain_2"].T)
    put("att_k_gain", a["att_k_gain_2"].T)
    put("ml_conv_w", a["ml_conv_w_2"].reshape(3, 8, P).transpose(2, 1, 0).reshape(P, -1))
    put("ml_conv_b", by_feature(a["ml_conv_b_2"]))
    put("ml_norm_g", by_feature(a["ml_norm_g_2"]))
    b = a["ml_gate_b_2"].reshape(4, 4)
    for name, (fwd, bwd) in (("ml_bias_i", (0, 2)), ("ml_bias_f", (1, 3))):
        par[0:4, PARAM_AT[name]] = b[fwd]
        par[32:36, PARAM_AT[name]] = b[bwd]
    both = np.stack([a["c_2"].reshape(KD, P), a["c_ctx_2"].reshape(KD, P)], 0)
    put("cond", both.transpose(2, 1, 0).reshape(P, -1))
    f["params"] = par
    f["consts"], f["mla_consts"], f["ml_consts"], f["gqa_rope"] = constants()
    return {n: np.ascontiguousarray(v) for n, v in f.items()}


def kernel(**inputs):
    import concourse.bacc as bacc
    from concourse.bass_utils import run_bass_kernel_spmd

    laid = _lay_out({n: np.asarray(v) for n, v in inputs.items()})
    nc = bacc.Bacc("TRN2", target_bir_lowering=False, num_devices=1)
    dram = {n: nc.dram_tensor(f"in_{n}", v.shape, mybir.dt.from_np(v.dtype), kind="ExternalInput").ap()
            for n, v in laid.items()}
    out = nc.dram_tensor("out_y", (P, KD, T), F32, kind="ExternalOutput").ap()
    build_blocks(nc, dram, out)
    r = run_bass_kernel_spmd(nc, [{f"in_{n}": v for n, v in laid.items()}], core_ids=[0])
    y = np.asarray(r.results[0]["out_y"])
    return y.transpose(1, 0, 2).reshape(D, T).T.reshape(1, T, D)
```
